# Optimizing a Trainium2 kernel written in Bass

```python
import jax, jax.numpy as jnp
from jax import lax
import numpy as np

D_MODEL = 2048
BATCH = 1
SEQ = 1024
DEPTH = 1

D_MIX = D_MODEL
RWKV_WIDTH = D_MIX // 2
SB_WIDTH = D_MIX - RWKV_WIDTH
HEAD_DIM = 64
RWKV_HEADS = RWKV_WIDTH // HEAD_DIM
SB_HEADS = SB_WIDTH // HEAD_DIM
DECAY_LORA = 64
ICLR_LORA = 64
PLE_DIM = 256
SB_BLOCK = 128
RMS_EPS = 1e-6
LNX_EPS = 64e-5
L2_EPS = 1e-12
SHIFT_WIDTH = 3 * RWKV_WIDTH + DECAY_LORA + ICLR_LORA
IN_WIDTH = SHIFT_WIDTH + RWKV_WIDTH + 4 * SB_WIDTH

kernel_name = "hymba_rwkv7_stickbreaking_layer"

def rms_norm(x, gain):
    xf = x.astype(jnp.float32)
    y = xf * lax.rsqrt(jnp.mean(xf * xf, axis=-1, keepdims=True) + RMS_EPS)
    return (y * gain.astype(jnp.float32)).astype(x.dtype)

def token_shift(u, mu):
    u_prev = jnp.pad(u, ((0, 0), (1, 0), (0, 0)))[:, :-1]
    return u + (u_prev - u) * mu

def split_heads(t):
    b, s, w = t.shape
    return t.reshape(b, s, w // HEAD_DIM, HEAD_DIM)

def rwkv7_scan(r, decay, k, v, kk, a):
    b, s, h, n = r.shape

    def step(state, inp):
        r_t, w_t, k_t, v_t, kk_t, a_t = inp
        sa = jnp.einsum('bhvk,bhk->bhv', state, kk_t)
        state = (state * w_t[:, :, None, :]
                 - sa[..., None] * (a_t * kk_t)[:, :, None, :]
                 + v_t[..., None] * k_t[:, :, None, :])
        y_t = jnp.einsum('bhvk,bhk->bhv', state, r_t)
        return state, y_t

    xs = (r.transpose(1, 0, 2, 3), decay.transpose(1, 0, 2, 3), k.transpose(1, 0, 2, 3),
          v.transpose(1, 0, 2, 3), kk.transpose(1, 0, 2, 3), a.transpose(1, 0, 2, 3))
    s0 = jnp.zeros((b, h, n, n), jnp.float32)
    _, y = lax.scan(step, s0, xs)
    return y.transpose(1, 0, 2, 3)

def rwkv7_time_mix(u_shift, g_lin, w0, w_up, a0, a_up, k_k, k_a, r_k, lnx_w, lnx_b):
    f32 = jnp.float32
    W = RWKV_WIDTH
    u = u_shift.astype(f32)
    r = u[..., :W]
    k = u[..., W:2 * W]
    v = u[..., 2 * W:3 * W]
    wd = u[..., 3 * W:3 * W + DECAY_LORA]
    ad = u[..., 3 * W + DECAY_LORA:]
    w_log = -jax.nn.softplus(-(w0.astype(f32) + jnp.tanh(wd) @ w_up.astype(f32))) - 0.5
    decay = jnp.exp(-jnp.exp(w_log))
    a = jax.nn.sigmoid(a0.astype(f32) + ad @ a_up.astype(f32))
    kk = split_heads(k * k_k.astype(f32))
    kk = kk * lax.rsqrt(jnp.sum(kk * kk, axis=-1, keepdims=True) + L2_EPS)
    k = k * (1.0 + (a - 1.0) * k_a.astype(f32))
    rh, kh, vh = split_heads(r), split_heads(k), split_heads(v)
    y = rwkv7_scan(rh, split_heads(decay), kh, vh, kk, split_heads(a))
    mean = jnp.mean(y, axis=-1, keepdims=True)
    var = jnp.mean(jnp.square(y - mean), axis=-1, keepdims=True)
    y = (y - mean) * lax.rsqrt(var + LNX_EPS)
    b, s = y.shape[:2]
    y = y.reshape(b, s, W) * lnx_w.astype(f32) + lnx_b.astype(f32)
    bonus = jnp.sum(rh * kh * split_heads(jnp.broadcast_to(r_k.astype(f32), r.shape)), axis=-1, keepdims=True) * vh
    y = y + bonus.reshape(b, s, W)
    return y * jax.nn.silu(g_lin.astype(f32))

def stick_breaking_attention(q, k, v):
    f32 = jnp.float32
    scale = HEAD_DIM ** -0.5
    qh = q.astype(f32).transpose(0, 2, 1, 3)
    kh = k.astype(f32).transpose(0, 2, 1, 3)
    vh = v.astype(f32).transpose(0, 2, 1, 3)
    s_len = qh.shape[2]
    outs = []
    for blk in range(s_len // SB_BLOCK):
        t0 = blk * SB_BLOCK
        end = t0 + SB_BLOCK
        qb = qh[:, :, t0:end]
        kb = kh[:, :, :end]
        vb = vh[:, :, :end]
        z = jnp.einsum('bhqd,bhkd->bhqk', qb, kb) * scale
        t_pos = t0 + jnp.arange(SB_BLOCK)[:, None]
        s_pos = jnp.arange(end)[None, :]
        strict = s_pos < t_pos
        log_beta = jax.nn.log_sigmoid(z)
        log_1mb = jnp.where(strict, jax.nn.log_sigmoid(-z), 0.0)
        suffix = lax.cumsum(log_1mb, axis=3, reverse=True) - log_1mb
        attn = jnp.where(strict, jnp.exp(log_beta + suffix), 0.0)
        outs.append(jnp.einsum('bhqk,bhkd->bhqd', attn, vb))
    o = jnp.concatenate(outs, axis=2)
    b = o.shape[0]
    return o.transpose(0, 2, 1, 3).reshape(b, s_len, SB_HEADS * HEAD_DIM)

def setup_inputs(seed: int = 0) -> dict:
    key = jax.random.key(seed)
    ks = jax.random.split(key, 20)
    f32 = jnp.float32
    nrm = lambda k, shape, s: jax.random.normal(k, shape, f32) * s
    return {
        "x": nrm(ks[0], (BATCH, SEQ, D_MODEL), 1.0),
        "p": nrm(ks[1], (DEPTH, BATCH, SEQ, PLE_DIM), 1.0),
        "g_pre": 1.0 + nrm(ks[2], (DEPTH, D_MODEL), 0.1),
        "w_in": nrm(ks[3], (DEPTH, D_MODEL, IN_WIDTH), D_MODEL ** -0.5),
        "mu_shift": jax.random.uniform(ks[4], (DEPTH, SHIFT_WIDTH), f32),
        "w0": jax.random.uniform(ks[5], (DEPTH, RWKV_WIDTH), f32, -4.0, 0.0),
        "w_up": nrm(ks[6], (DEPTH, DECAY_LORA, RWKV_WIDTH), 0.5 * DECAY_LORA ** -0.5),
        "a0": nrm(ks[7], (DEPTH, RWKV_WIDTH), 0.1),
        "a_up": nrm(ks[8], (DEPTH, ICLR_LORA, RWKV_WIDTH), 0.5 * ICLR_LORA ** -0.5),
        "k_k": 0.85 + nrm(ks[9], (DEPTH, RWKV_WIDTH), 0.05),
        "k_a": 1.0 + nrm(ks[10], (DEPTH, RWKV_WIDTH), 0.05),
        "r_k": nrm(ks[11], (DEPTH, RWKV_WIDTH), 0.1),
        "lnx_w": 1.0 + nrm(ks[12], (DEPTH, RWKV_WIDTH), 0.1),
        "lnx_b": nrm(ks[13], (DEPTH, RWKV_WIDTH), 0.02),
        "w_out": nrm(ks[14], (DEPTH, D_MIX, D_MODEL), D_MIX ** -0.5),
        "g_post": 1.0 + nrm(ks[15], (DEPTH, D_MODEL), 0.1),
        "w_ple": nrm(ks[16], (DEPTH, PLE_DIM, D_MODEL), PLE_DIM ** -0.5),
        "w_plg": nrm(ks[17], (DEPTH, D_MODEL, D_MODEL), D_MODEL ** -0.5),
        "g_ple": 1.0 + nrm(ks[18], (DEPTH, D_MODEL), 0.1),
    }

def reference(x, p, g_pre, w_in, mu_shift, w0, w_up, a0, a_up, k_k, k_a, r_k,
              lnx_w, lnx_b, w_out, g_post, w_ple, w_plg, g_ple):
    h = x
    for i in range(DEPTH):
        xn = rms_norm(h, g_pre[i])
        u = xn @ w_in[i]
        u_shift = token_shift(u[..., :SHIFT_WIDTH], mu_shift[i])
        o = SHIFT_WIDTH
        g_rwkv = u[..., o:o + RWKV_WIDTH]; o += RWKV_WIDTH
        q_sb = u[..., o:o + SB_WIDTH]; o += SB_WIDTH
        k_sb = u[..., o:o + SB_WIDTH]; o += SB_WIDTH
        v_sb = u[..., o:o + SB_WIDTH]; o += SB_WIDTH
        g_sb = u[..., o:o + SB_WIDTH]
        y_a = rwkv7_time_mix(u_shift, g_rwkv, w0[i], w_up[i], a0[i], a_up[i],
                             k_k[i], k_a[i], r_k[i], lnx_w[i], lnx_b[i])
        y_b = stick_breaking_attention(split_heads(q_sb), split_heads(k_sb), split_heads(v_sb))
        y_b = y_b * jax.nn.silu(g_sb.astype(jnp.float32))
        mix = jnp.concatenate([y_a, y_b], axis=-1).astype(h.dtype) @ w_out[i]
        h = h + rms_norm(mix, g_post[i])
        ple = rms_norm(p[i] @ w_ple[i], g_ple[i])
        h = h + ple * jax.nn.sigmoid(h @ w_plg[i])
    return h


_drawn_inputs = setup_inputs


def setup_inputs(seed=0):
    import zlib

    import numpy as np

    out = dict(_drawn_inputs(seed))
    spreads = {}
    factors = {'k_k': 3.941, 'lnx_b': 5.009}
    for name, (base, spread) in spreads.items():
        noise = np.random.default_rng([zlib.crc32(name.encode()), seed]).standard_normal(out[name].shape)
        drawn = base * np.exp(spread * noise) if base else spread * noise
        out[name] = __import__('jax').numpy.asarray(drawn.astype(out[name].dtype))
    for name, factor in factors.items():
        out[name] = (out[name] * factor).astype(out[name].dtype)
    return out
```

```python
from contextlib import ExitStack

import numpy as np

import concourse.bass as bass
from concourse import mybir

F32 = mybir.dt.float32
F32R = mybir.dt.float32r
ALU = mybir.AluOpType
ACT = mybir.ActivationFunctionType
AX_X = mybir.AxisListType.X

P = 128
HD = 64
HALF = 512
RMS_EPS = 1e-6
LNX_EPS = 64e-5
L2_EPS = 1e-12


def layer_kernel(nc, x, p, g_pre, w_in, mu_shift, w0, w_up, a0, a_up, k_k, k_a, r_k,
                 lnx_w, lnx_b, w_out, g_post, w_ple, w_plg, g_ple, out):
    S, D = x.shape[1], x.shape[2]
    W = w0.shape[1]
    IN_W = w_in.shape[2]
    PLE = p.shape[3]
    KT = D // P
    TB = S // P
    NPAIR = W // P
    HB = HALF // P
    CH = 64
    QK = 4
    LORA = 3 * NPAIR
    assert S == 2 * HALF and D == 2 * W and IN_W == (8 * NPAIR + 1) * P

    x_rows = x[0].rearrange("(b p) d -> p b d", p=P)
    out_rows = out[0].rearrange("(b p) d -> p b d", p=P)
    p_rows = p[0, 0].rearrange("(b p) d -> p b d", p=P)
    w_out_t = w_out[0].rearrange("(k p) n -> p k n", p=P)
    w_ple_t = w_ple[0].rearrange("(k p) n -> p k n", p=P)
    w_plg_t = w_plg[0].rearrange("(k p) n -> p k n", p=P)
    NC = 2 * (KT // 2) * (D // HALF) + D // HALF
    w_in_t = w_in[0].rearrange("(k p) n -> p k n", p=P)

    vectors = [("g_pre", g_pre), ("mu", mu_shift), ("w0", w0), ("a0", a0), ("k_k", k_k), ("k_a", k_a),
               ("r_k", r_k), ("lnx_w", lnx_w), ("lnx_b", lnx_b)]
    vec_at, NVEC = {}, 0
    for name, v in vectors:
        vec_at[name] = NVEC
        NVEC += v.shape[1] // P

    u_t = nc.dram_tensor("u_t", (IN_W, S), F32, kind="Internal").ap()
    mix_t = nc.dram_tensor("mix_t", (D, S), F32, kind="Internal").ap()

    mix_tt = mix_t.rearrange("(k p) s -> p k s", p=P)
    assert PLE == 2 * P and D == 4 * HALF

    with ExitStack() as ctx:
        def sb(name, shape, dt=F32, c=ctx):
            return c.enter_context(nc.sbuf_tensor(name, shape, dt))

        def sem(name):
            return ctx.enter_context(nc.semaphore(name))

        ps = ctx.enter_context(nc.psum_tensor("ps", [P, 8, HALF], F32))
        banks = [ps[:, i] for i in range(8)]

        ident = sb("ident", [P, P])
        vec_rows = sb("vec_rows", [NVEC, P])
        tick = sb("tick", [P, 2])
        vec_cols = sb("vec_cols", [P, NVEC])

        def vec(name, b):
            return vec_cols[:, vec_at[name] + b:vec_at[name] + b + 1]

        with ExitStack() as c1:
            xh = sb("xh", [P, KT, S], F32R, c1)
            xl = sb("xl", [P, KT, S], F32R, c1)
            with ExitStack() as c0:
                x_in = sb("x_in", [P, HB, D], F32, c0)
                sq_junk = sb("sq_junk", [P, D], F32, c0)
                ms = sb("ms", [P, TB], F32, c0)
                rstd = sb("rstd", [P, TB], F32, c0)
            w_raw = sb("w_raw", [P, 2, QK, P], F32, c1)
            wh = sb("wh", [P, 2, QK, P], F32R, c1)
            wl = sb("wl", [P, 2, QK, P], F32R, c1)
            u_stage = sb("u_stage", [P, 2, HALF], F32, c1)
            with ExitStack() as ca:
                raw_q = sb("raw_q", [P, 2, HALF], F32, ca)
                qh = sb("qh", [P, S], F32R, ca)
                ql = sb("ql", [P, S], F32R, ca)
                kh = sb("kh", [P, S], F32R, ca)
                kl = sb("kl", [P, S], F32R, ca)
                vth = sb("vth", [P, TB, P], F32R, ca)
                vtl = sb("vtl", [P, TB, P], F32R, ca)
                e_t = sb("e_t", [P, 3, HALF], F32, ca)
                r_t = sb("r_t", [P, 2, HALF], F32, ca)
                rh = sb("rh", [P, 3, HALF], F32R, ca)
                rl = sb("rl", [P, 3, HALF], F32R, ca)
                pah = sb("pah", [P, 2, HALF], F32R, ca)
                pal = sb("pal", [P, 2, HALF], F32R, ca)
                c_raw = sb("c_raw", [P, 4, P], F32, ca)
                c_r = sb("c_r", [P, 4, P], F32R, ca)
            with ExitStack() as cr:
                la = sb("la", [P, S], F32, cr)
                lw = sb("lw", [P, P], F32, cr)
                pc = sb("pc", [P, 12], F32, cr)
                m_r = sb("m_r", [P, 9, P], F32, cr)
                zero_r = sb("zero_r", [P, CH], F32, cr)
                ld = sb("ld", [P, 3, HALF + 4], F32, cr)
                rkv = sb("rkv", [P, 3, HALF], F32, cr)
                tt = sb("tt", [P, 6, HALF], F32, cr)
                yb = sb("yb", [P, HALF], F32, cr)
                n_t = sb("n_t", [P, 4, P], F32, cr)
                arb = sb("arb", [P, 4, P], F32, cr)
                aak = sb("aak", [P, 4, P], F32, cr)
                ark = sb("ark", [P, 4, P], F32, cr)
                nb = sb("nb", [P, 2, 4, P], F32, cr)
                z_t = sb("z_t", [P, 4, P], F32, cr)
                u_i = sb("u_i", [P, 4, P], F32, cr)
                t_i = sb("t_i", [P, 4, P], F32, cr)
                tok = sb("tok", [P, 4, 2, P], F32, cr)
                x_t = sb("x_t", [P, 4, HD], F32, cr)
                up = sb("up", [P, 2, P], F32, cr)
                wt = sb("wt", [P, 2, P], F32, cr)
                sa = sb("sa", [P, 2, P], F32, cr)
                st = sb("st", [P, 2, P], F32, cr)
            raw_k = e_t[:, 0:2].rearrange("p a n -> p (a n)")
            raw_la = ld[:, :, :].rearrange("p a n -> p (a n)")
            la_d = rkv[:, 0:2].rearrange("p a n -> p (a n)")
            raw_v = r_t[:, 0:2].rearrange("p a n -> p (a n)")

        with ExitStack() as c3:
            ah = sb("ah", [P, KT, HALF], F32R, c3)
            al = sb("al", [P, KT, HALF], F32R, c3)
            rows = sb("rows", [P, HB, D], F32, c3)
            ple = sb("ple", [P, HB, D], F32, c3)
            v_raw = sb("v_raw", [P, 4, 2, HALF], F32, c3)
            vh = sb("vh", [P, 2, 2, HALF], F32R, c3)
            vl = sb("vl", [P, 2, 2, HALF], F32R, c3)
            g_post_b = sb("g_post_b", [P, D], F32, c3)
            g_ple_b = sb("g_ple_b", [P, D], F32, c3)
            x_res = sb("x_res", [P, D], F32, c3)
            p_in = sb("p_in", [P, HB, PLE], F32, c3)
            ph = sb("ph", [P, PLE // P, HALF], F32R, c3)
            pl = sb("pl", [P, PLE // P, HALF], F32R, c3)
            m_in = sb("m_in", [P, 2, 2, HALF], F32, c3)
            ss = sb("ss", [P, 2, HB, 4], F32, c3)
            rs = sb("rs", [P, 2, HB], F32, c3)
            sq_out = sb("sq_out", [P, HALF], F32, c3)
        NP_ = 12
        LAST = [7, 15, 23, 31, 32, 33, 34, 35, 43, 51, 59, 67]
        sg = [m_in[:, i // 2, i % 2] for i in range(4)]

        s_ident0 = sem("s_ident0")
        s_ident = sem("s_ident")
        s_vec = sem("s_vec")
        s_vect = sem("s_vect")
        s_vcol = sem("s_vcol")
        s_x = [sem(f"s_x{b}") for b in range(HB)]
        s_sq = sem("s_sq")
        s_ln = sem("s_ln")
        s_rstd = sem("s_rstd")
        s_xn = sem("s_xn")
        s_xt = sem("s_xt")
        s_xh = sem("s_xh")
        s_xl = sem("s_xl")
        s_w = [sem(f"s_w{i}") for i in range(2)]
        s_wh = sem("s_wh")
        s_wl = sem("s_wl")
        s_wused = sem("s_wused")
        s_ulo = sem("s_ulo")
        s_uhi = sem("s_uhi")
        s_ust = [sem(f"s_ust{i}") for i in range(2)]

        s_c0 = sem("s_c0")
        s_c1 = sem("s_c1")
        s_c2 = sem("s_c2")
        s_qkv = [sem(f"s_qkv{i}") for i in range(3)]
        s_th = sem("s_th")
        s_tl = sem("s_tl")
        s_vt = sem("s_vt")
        s_z = sem("s_z")
        s_a1 = sem("s_a1")
        s_sp = sem("s_sp")
        s_dm = sem("s_dm")
        s_r = sem("s_r")
        s_rh = sem("s_rh")
        s_rl = sem("s_rl")
        s_arg = sem("s_arg")
        s_ex = sem("s_ex")
        s_ah = sem("s_ah")
        s_al = sem("s_al")
        s_pv = sem("s_pv")
        s_y = sem("s_y")
        s_g = sem("s_g")
        s_ga = sem("s_ga")
        s_gd = sem("s_gd")
        s_gp = sem("s_gp")
        s_mst = sem("s_mst")

        s_la = sem("s_la")
        s_lo1 = sem("s_lo1")
        s_lo = sem("s_lo")
        s_msk = sem("s_msk")
        s_rld = sem("s_rld")
        s_lw = sem("s_lw")
        s_z0 = sem("s_z0")
        s_rg = sem("s_rg")
        s_rst = sem("s_rst")
        s_pre = {e: sem(f"s_pre_{e}") for e in ("act", "dve", "pe")}
        s_quad = {e: sem(f"s_quad_{e}") for e in ("act", "dve", "pe", "pool")}
        s_post = {e: sem(f"s_post_{e}") for e in ("act", "dve", "pe")}

        s_gb = sem("s_gb")
        s_m = [sem(f"s_m{i}") for i in range(2)]
        s_mh = sem("s_mh")
        s_ml = sem("s_ml")
        s_v = [sem(f"s_v{i}") for i in range(4)]
        s_vh = sem("s_vh")
        s_vl = sem("s_vl")
        s_vused = sem("s_vused")
        s_ev01 = sem("s_ev01")
        s_ev23 = sem("s_ev23")
        s_ss = sem("s_ss")
        s_sum = sem("s_sum")
        s_rln = sem("s_rln")
        s_rs = sem("s_rs")
        s_gain = sem("s_gain")
        s_xr = sem("s_xr")
        s_h = sem("s_h")
        s_p = sem("s_p")
        s_pt = sem("s_pt")
        s_ph = sem("s_ph")
        s_pl = sem("s_pl")
        s_ht = sem("s_ht")
        s_hh = sem("s_hh")
        s_hl = sem("s_hl")
        s_sg = sem("s_sg")
        s_sgd = sem("s_sgd")
        s_out = sem("s_out")
        s_store = sem("s_store")

        block = ctx.enter_context(nc.Block())

        def need(eng, s, v):
            if not isinstance(v, int) or v > 0:
                eng.wait_ge(s, v)

        SB_COLS = [4 * NPAIR + 1, 5 * NPAIR + 1, 6 * NPAIR + 1, 7 * NPAIR + 1]
        RW_COLS = [0, NPAIR, 2 * NPAIR, 3 * NPAIR + 1]
        N0 = 5
        NPAN = 8 * NPAIR + 1
        UNITS = [(Q, e, b) for Q in range(2) for e in range(2) for b in range(4 * Q + 3, -1, -1)]
        NU = len(UNITS)
        first = [b == 4 * Q + 3 for Q, e, b in UNITS]
        last = [b == 0 for Q, e, b in UNITS]
        diag = [b >= 4 * Q for Q, e, b in UNITS]
        lo = [P * (b - 4 * Q) if b >= 4 * Q else 0 for Q, e, b in UNITS]
        lo2 = [lo[n] + (P if diag[n] else 0) for n in range(NU)]
        n_diag = [sum(diag[:n + 1]) for n in range(NU)]
        n_add = [sum(not f for f in first[:n + 1]) for n in range(NU)]
        chain = [2 * Q + e for Q, e, b in UNITS]
        PRE, SLOTS = 10, NU + 4

        LV = 5
        PRE_STEPS = {
            "dve": "c1 c2 c3 z d r k v wm ws am as scan cp kkn At akk Bh kt k2 rk Kh Rt Kb Bb bon".split(),
            "act": "w1 a1 w2 a2 w3 a3 w4 a4 sq P Pp Pi rn1 rn2".split(),
            "pe": "xw xa ss bs".split()}
        QUAD_STEPS = {
            "pe": ["gN", "gB", "gA", "gK", "tr1", "tr2"] + [f"{w}{l}" for l in range(LV) for w in "zv"]
                  + ["x", "wt", "uu"] + [f"{w}{c}" for c in range(4) for w in ("sa", "st")] + ["y"],
            "dve": ["N", "n1", "u", "t", "B", "A", "K"] + [w + str(l) for l in range(LV) for w in "ut" if w == "u" or l < LV - 1]
                   + [f"{w}{c}" for c in range(4) for w in ("sa", "st")],
            "act": ["tc1", "tc2"] + [f"z{l}" for l in range(LV)] + ["xc", "wc", "uc", "y"],
            "pool": [f"nb{l}" for l in range(LV)]}
        QUAD_STEPS["pe"] = [x for x in QUAD_STEPS["pe"] if x != "x"]
        QUAD_STEPS["pe"].insert(6, "x")
        QUAD_STEPS["act"] = ["tc1", "tc2", "xc"] + [f"z{l}" for l in range(LV)] + ["wc", "uc", "y"]
        POST_STEPS = {"pe": ["m", "vv"], "act": "g1 g2 g3 g4 q l e".split(), "dve": "gm gg yc yn yw yb out".split()}

        def after(eng, sems, steps, who, name, n):
            eng.wait_ge(sems[who], n * len(steps[who]) + steps[who].index(name) + 1)

        M_STRICT, M_FULL, M_ONES, M_PAIR, M_LEV = 0, 1, 2, 3, 4
        K_MASK = 3 + 3 * 2 + 2 + (LV + 1) * 4
        RW0 = N0 + 4 * NPAIR

        def tiles_by(t, part):
            if t < 0:
                return PRE
            return PRE + (64 - PRE) * min(3 * t + part + 1, 3 * SLOTS - 3) // (3 * SLOTS - 3)

        def load_quarter(sp, col, p_, q):
            need(sp, s_wl, 4 * p_ + q - 1)
            sp.dma_start(w_raw[:, q % 2], w_in_t[:, q * QK:(q + 1) * QK, bass.ds(col * P, P)]).then_inc(s_w[q % 2], 16)

        def store_panel(sp, col, p_):
            sp.wait_ge(s_ulo, p_ + 1)
            sp.dma_start(u_t[bass.ds(col * P, P), 0:HALF], u_stage[:, 0]).then_inc(s_ust[0], 16)
            sp.wait_ge(s_uhi, p_ + 1)
            sp.dma_start(u_t[bass.ds(col * P, P), HALF:S], u_stage[:, 1]).then_inc(s_ust[1], 16)

        def group_io(sp, cols, p_, before):
            for j in range(16):
                load_quarter(sp, cols[j // 4], p_ + j // 4, j % 4)
                if j % 4 == 2:
                    col = cols[j // 4 - 1] if j >= 4 else before
                    if col is not None:
                        store_panel(sp, col, p_ + j // 4 - 1)

        def split_high(act, p_, q):
            act.wait_ge(s_w[q % 2], 16 * (2 * p_ + q // 2 + 1))
            need(act, s_wused, 4 * p_ + q - 1)
            act.activation(wh[:, q % 2], w_raw[:, q % 2], ACT.Copy).then_inc(s_wh, 1)

        def split_low(dve, p_, q):
            dve.wait_ge(s_wh, 4 * p_ + q + 1)
            dve.tensor_tensor(wl[:, q % 2], w_raw[:, q % 2], wh[:, q % 2].bitcast(F32), ALU.subtract).then_inc(s_wl, 1)

        def panel_lo(act, p_, par):
            act.wait_ge(s_wused, 4 * p_ + 4)
            need(act, s_ust[0], 16 * p_)
            act.activation(u_stage[:, 0], banks[2 * par][:, :], ACT.Copy).then_inc(s_ulo, 1)

        def panel_hi(dve, p_, par):
            dve.wait_ge(s_wused, 4 * p_ + 4)
            need(dve, s_ust[1], 16 * p_)
            dve.tensor_copy(u_stage[:, 1], banks[2 * par + 1][:, :]).then_inc(s_uhi, 1)

        def project_tile(pe, p_, par, k):
            q = k // QK
            if k == 0:
                need(pe, s_ulo, p_ - 1)
                need(pe, s_uhi, p_ - 1)
            if k % QK == 0:
                pe.wait_ge(s_wl, 4 * p_ + q + 1)
            for n, (wt, xt) in enumerate(((wh, xh), (wh, xl), (wl, xh))):
                for t in range(2):
                    mm = pe.matmul(banks[2 * par + t][:, :], wt[:, q % 2, k % QK], xt[:, k, t * HALF:(t + 1) * HALF],
                                   start=(k == 0 and n == 0), stop=(k == KT - 1 and n == 2))
            if k % QK == QK - 1:
                mm.then_inc(s_wused, 1)

        def tiles(pe, p_, a, b):
            for j in range(a, b):
                project_tile(pe, p_ + j // KT, (1 + j // KT) % 2, j % KT)

        def rw_tile(h, stage, k):
            return 32 * h + (4 * k if stage == "pre" else 12 + 10 * stage + k)

        def split_upto(eng, split, evac, p_, a, b):
            for j in range(a, b + 1):
                if j % 4 == 0 and (j > a or b == 0) and j // 4 + 1 < 16:
                    for jq in ([0, 1] if j == 0 else [j // 4 + 1]):
                        split(eng, p_ + jq // 4, jq % 4)
                if j % KT == 0 and j > a:
                    evac(eng, p_ + j // KT - 1, (j // KT) % 2)

        @block.sync
        def _(sp):
            for h in range(2):
                for b in range(HB):
                    if h:
                        sp.wait_ge(s_xt, KT)
                    sp.dma_start(x_in[:, b], x_rows[:, h * HB + b]).then_inc(s_x[b], 16)
                if h == 0:
                    for name, v in vectors:
                        sp.dma_start(vec_rows[vec_at[name]:vec_at[name] + v.shape[1] // P, :],
                                     v[0].rearrange("(b c) -> b c", c=P)).then_inc(s_vec, 16)
            sp.wait_ge(s_xt, 2 * KT)

            group_io(sp, SB_COLS, 0, None)
            for q in range(4):
                load_quarter(sp, LORA, 4, q)
                if q == 2:
                    store_panel(sp, SB_COLS[3], 3)
            group_io(sp, [c + 1 for c in SB_COLS], N0, LORA)
            with sp.Fori(1, NPAIR - 1) as i:
                group_io(sp, [c + i + 1 for c in SB_COLS], N0 + 4 * i, SB_COLS[3] + i)
            group_io(sp, RW_COLS, N0 + 4 * (NPAIR - 1), SB_COLS[3] + NPAIR - 1)
            with sp.Fori(0, NPAIR - 1) as i:
                group_io(sp, [c + i + 1 for c in RW_COLS], N0 + 4 * NPAIR + 4 * i, RW_COLS[3] + i)
            store_panel(sp, RW_COLS[3] + NPAIR - 1, NPAN - 1)

            for t in range(2):
                sp.wait_ge(s_ust[t], 16 * (8 * NPAIR + 1))

            sp.wait_ge(s_wused, 4 * (8 * NPAIR + 1))
            sp.wait_ge(s_wl, 4 * (8 * NPAIR + 1))
            sp.wait_ge(s_ulo, 8 * NPAIR + 1)
            sp.wait_ge(s_uhi, 8 * NPAIR + 1)
            sp.wait_ge(s_mst, 32 * NPAIR)
            sp.wait_ge(s_rst, 32 * NPAIR)
            sp.dma_start(g_post_b[:, :], g_post[0:1, :].broadcast_to((P, D))).then_inc(s_gb, 16)
            sp.dma_start(g_ple_b[:, :], g_ple[0:1, :].broadcast_to((P, D))).then_inc(s_gb, 16)
            sp.nop().then_inc(s_store, 16)
            with sp.Fori(0, 2) as h:
                sp.wait_ge(s_store, 16 * 16 * h + 16)
                sp.wait_ge(s_vused, h * NC + 2)
                sp.wait_ge(s_pl, h * 2 + 1)
                sp.dma_start(p_in[:, :, :], p_rows[:, bass.ds(h * HB, HB), :]).then_inc(s_p, 16)

                def load_chunk(c):
                    if c < 32:
                        src = w_out_t[:, 2 * (c % 8):2 * (c % 8) + 2, c // 8 * HALF:(c // 8 + 1) * HALF]
                    elif c < 36:
                        src = w_ple_t[:, :, (c - 32) * HALF:(c - 31) * HALF]
                    else:
                        n, kk = (c - 36) // 8, (c - 36) % 8
                        src = w_plg_t[:, 2 * kk:2 * kk + 2, n * HALF:(n + 1) * HALF]
                    sp.wait_ge(s_vl, h * NC + c + 1)
                    sp.dma_start(v_raw[:, c % 4], src).then_inc(s_v[c % 4], 16)

                def store_tiles(n):
                    for b in range(HB):
                        sp.wait_ge(s_out, h * 16 + 4 * n + b + 1 + 4)
                        sp.dma_start(out_rows[:, h * HB + b, n * HALF:(n + 1) * HALF],
                                     rows[:, b, n * HALF:(n + 1) * HALF]).then_inc(s_store, 16)

                for m in range(KT // 2):
                    sp.wait_ge(s_ml, h * (KT // 2) + m + 1)
                    sp.dma_start(m_in[:, m % 2], mix_tt[:, 2 * m:2 * m + 2, bass.ds(h * HALF, HALF)]).then_inc(s_m[m % 2], 16)
                    if m < 4:
                        load_chunk(m)
                for c in range(4, NC):
                    load_chunk(c)
                    if c in (30, 35, 36, 37):
                        b = max(c - 34, 0)
                        sp.wait_ge(s_h, h * HB + b + 1)
                        sp.dma_start(x_res[:, :], x_rows[:, h * HB + b, :]).then_inc(s_xr, 16)
                    if c in (49, 57, 65):
                        store_tiles((c - 49) // 8)
                store_tiles(3)
            sp.wait_ge(s_store, 16 * 33)
            sp.wait_ge(s_gb, 32)

        @block.gpsimd
        def _(pool):
            pool.memset(ident[:, :], 0.0).then_inc(s_ident0, 1)
            pool.wait_ge(s_ident0, 1)
            pool.affine_select(out=ident[:, :], in_=ident[:, :], compare_op=ALU.not_equal, fill=1.0, base=0,
                               pattern=[[-1, P]], channel_multiplier=1).then_inc(s_ident, 1)
            pool.wait_ge(s_xl, 2 * KT)
            TILES = [(-1.0, ALU.is_ge, 1), (-1.0, ALU.is_gt, -1), (-2.0 ** 100, ALU.is_ge, 1), (1.0, ALU.is_gt, -1)]
            for n, (value, _, _) in enumerate(TILES):
                pool.memset(c_raw[:, n], value).then_inc(s_c0, 1)
            for n, (_, op, sign) in enumerate(TILES):
                pool.wait_ge(s_c0, n + 1)
                pool.affine_select(out=c_raw[:, n], in_=c_raw[:, n], compare_op=op, fill=0.0, base=0,
                                   pattern=[[-sign, P]], channel_multiplier=sign).then_inc(s_c1, 1)

            def sb_io(i):
                rows = D // 2 + i * P
                for t in range(2):
                    pool.wait_ge(s_ust[t], 16 * (N0 + 4 * i))
                for n, dst in enumerate((raw_q[:, :, :].rearrange("p a n -> p (a n)"), raw_k, raw_v)):
                    pool.dma_start(dst, u_t[bass.ds((SB_COLS[n] + i) * P, P), :]).then_inc(s_qkv[n], 16)
                for Q in range(2):
                    if Q == 0:
                        pool.wait_ge(s_tl, 4 * i + 1)
                    else:
                        pool.wait_ge(s_mst, 32 * i + 16)
                    pool.dma_start(raw_q[:, 0], u_t[bass.ds((SB_COLS[3] + i) * P, P), Q * HALF:(Q + 1) * HALF]).then_inc(s_g, 16)
                    pool.wait_ge(s_ga, 8 * i + 4 * Q + 4)
                    pool.tensor_tensor(raw_q[:, 1], raw_q[:, 0], raw_q[:, 1], ALU.mult).then_inc(s_gp, 1)
                    pool.wait_ge(s_y, 4 * i + 2 * Q + 2)
                    pool.dma_start(mix_t[bass.ds(rows, P), Q * HALF:(Q + 1) * HALF], raw_q[:, 1]).then_inc(s_mst, 16)
                pool.wait_ge(s_mst, 32 * i + 32)

            with pool.Fori(0, NPAIR - 1) as i:
                sb_io(i)
            sb_io(NPAIR - 1)

            pool.wait_ge(s_c2, 2)
            k_ = 0
            pool.memset(zero_r[:, :], 0.0).then_inc(s_msk, 1)
            pool.memset(m_r[:, :, :], 1.0).then_inc(s_msk, 1)
            pool.memset(tick[:, :], 0.0)
            pool.memset(st[:, :, :], 0.0).then_inc(s_msk, 1)
            k_ = 3

            def select(tile, pattern, base, cm, op):
                nonlocal k_
                pool.wait_ge(s_msk, k_)
                v = tile
                pool.affine_select(out=v, in_=v, compare_op=op, fill=0.0, base=base, pattern=pattern,
                                   channel_multiplier=cm).then_inc(s_msk, 1)
                k_ += 1

            def same_block(tile, width):
                v = tile.rearrange("p (c t) -> p c t", t=width)
                select(v, [[-width, P // width], [0, width]], 0, 1, ALU.is_ge)
                select(v, [[width, P // width], [0, width]], width - 1, -1, ALU.is_ge)

            for m in (M_STRICT, M_FULL, M_ONES):
                same_block(m_r[:, m], CH)
            select(m_r[:, M_STRICT], [[1, P]], 0, -1, ALU.is_gt)
            select(m_r[:, M_FULL], [[1, P]], 0, -1, ALU.is_ge)
            for l in range(LV + 1):
                b = 1 << l
                m = m_r[:, M_PAIR + l]
                same_block(m, 2 * b)
                v = m.rearrange("p (c h t) -> p c h t", h=2, t=b)
                select(v, [[2 * b, P // (2 * b)], [0, 2], [0, b]], b, -1, ALU.is_gt)
                select(v, [[0, P // (2 * b)], [1, 2], [0, b]], 0, 0, ALU.is_gt)

            pool.wait_ge(s_msk, k_)
            for t in range(2):
                pool.wait_ge(s_ust[t], 16 * N0)
            pool.dma_start(raw_la[:, 0:S], u_t[LORA * P:LORA * P + P, :]).then_inc(s_la, 16)

            def rw_io(i):
                for t in range(2):
                    pool.wait_ge(s_ust[t], 16 * (RW0 + 4 * i))
                pool.dma_start(lw[0:HD, :], w_up[0][:, bass.ds(i * P, P)]).then_inc(s_lw, 16)
                pool.dma_start(lw[HD:P, :], a_up[0][:, bass.ds(i * P, P)]).then_inc(s_lw, 16)
                for h in range(2):
                    r = 2 * i + h
                    if h == 0:
                        pool.memset(ld[:, :, 3:4], 0.0).then_inc(s_z0, 1)
                    for n in range(3):
                        row = (RW_COLS[n] + i) * P
                        if h == 0:
                            pool.dma_start(ld[:, n, 4:4 + HALF], u_t[bass.ds(row, P), 0:HALF]).then_inc(s_rld, 16)
                        else:
                            pool.dma_start(ld[:, n, 3:4 + HALF], u_t[bass.ds(row, P), HALF - 1:S]).then_inc(s_rld, 16)
                    after(pool, s_pre, PRE_STEPS, "dve", "v", r)
                    pool.dma_start(ld[:, 0, 0:HALF], u_t[bass.ds((RW_COLS[3] + i) * P, P), h * HALF:(h + 1) * HALF]).then_inc(s_rg, 16)
                    for qd in range(2):
                        n = 2 * r + qd
                        after(pool, s_quad, QUAD_STEPS, "dve", "N", n)
                        for l in range(LV):
                            if l >= 2:
                                after(pool, s_quad, QUAD_STEPS, "pe", f"z{l - 2}", n)
                            pool.tensor_tensor(nb[:, l % 2], n_t[:, :, :], m_r[:, M_LEV + l:M_LEV + l + 1].broadcast_to((P, 4, P)),
                                               ALU.mult).then_inc(s_quad["pool"], 1)
                    after(pool, s_post, POST_STEPS, "dve", "out", r)
                    pool.tensor_tensor(tick[:, 1:2], tick[:, 0:1], tick[:, 0:1], ALU.add)
                    pool.dma_start(mix_t[bass.ds(i * P, P), h * HALF:(h + 1) * HALF], yb[:, :]).then_inc(s_rst, 16)
                    pool.wait_ge(s_rst, 16 * (r + 1))

            pool.wait_ge(s_lo, 3)
            with pool.Fori(0, NPAIR - 1) as i:
                rw_io(i)
            rw_io(NPAIR - 1)

        @block.scalar
        def _(act):
            act.preload_act_table_set("natural_log_exp_and_others")
            for h in range(2):
                for b in range(HB):
                    n = h * HB + b
                    act.wait_ge(s_x[b], 16 * (h + 1))
                    if n:
                        act.wait_ge(s_sq, n)
                    act.activation(sq_junk[:, :], x_in[:, b], ACT.Square, accum_out=ms[:, n:n + 1]).then_inc(s_sq, 1)
                    act.wait_ge(s_sq, n + 1)
                    act.activation(rstd[:, n:n + 1], ms[:, n:n + 1], ACT.Ln, bias=RMS_EPS, scale=1.0 / D).then_inc(s_ln, 1)
                    act.wait_ge(s_ln, n + 1)
                    act.activation(rstd[:, n:n + 1], rstd[:, n:n + 1], ACT.Exp, scale=-0.5).then_inc(s_rstd, 1)
                if h == 0:
                    act.wait_ge(s_vect, 1)
                    act.activation(vec_cols[:, :], banks[4][:, 0:NVEC], ACT.Copy).then_inc(s_vcol, 1)
                    act.wait_ge(s_vcol, 1)
                for k in range(KT):
                    act.wait_ge(s_xt, h * KT + k + 1)
                    act.activation(xh[:, k, h * HALF:(h + 1) * HALF], banks[k % 4][:, :], ACT.Copy,
                                   scale=vec("g_pre", k)).then_inc(s_xh, 1)

            for p_ in range(N0):
                for q in range(4):
                    split_high(act, p_, q)
                    if q == 1 and p_:
                        panel_lo(act, p_ - 1, (p_ - 1) % 2)
            panel_lo(act, N0 - 1, 0)
            act.wait_ge(s_c1, 4)
            act.activation(c_r[:, 0:3], c_raw[:, 0:3], ACT.Copy).then_inc(s_c2, 1)
            act.activation(c_r[:, 3], ident[:, :], ACT.Copy).then_inc(s_c2, 1)

            def sb_act(i, p_):
                U, due = NU * i, lambda a, b: split_upto(act, split_high, panel_lo, p_, a, b)

                def gate_step(Q, step):
                    done = 8 * i + 4 * Q
                    if step == 0:
                        act.wait_ge(s_g, 16 * (2 * i + Q + 1))
                        act.activation(raw_q[:, 1], raw_q[:, 0], ACT.Abs).then_inc(s_ga, 1)
                    elif step == 1:
                        act.wait_ge(s_ga, done + 1)
                        act.activation(raw_q[:, 1], raw_q[:, 1], ACT.Exp, scale=-1.0).then_inc(s_ga, 1)
                    elif step == 2:
                        act.wait_ge(s_ga, done + 2)
                        act.activation(raw_q[:, 1], raw_q[:, 1], ACT.Ln, bias=1.0).then_inc(s_ga, 1)
                    else:
                        act.wait_ge(s_gd, 2 * i + Q + 1)
                        act.activation(raw_q[:, 1], raw_q[:, 1], ACT.Exp).then_inc(s_ga, 1)

                due(0, 0)
                due(0, PRE)
                act.wait_ge(s_qkv[0], 16 * (i + 1))
                act.activation(qh[:, :], raw_q[:, :, :].rearrange("p a n -> p (a n)"), ACT.Copy, scale=HD ** -0.5).then_inc(s_th, 1)
                act.wait_ge(s_qkv[1], 16 * (i + 1))
                act.activation(kh[:, :], raw_k, ACT.Copy).then_inc(s_th, 1)
                for m in range(2):
                    act.wait_ge(s_vt, 2 * i + m + 1)
                    act.activation(vth[:, 4 * m:4 * m + 4, :], banks[4 + m][:, :], ACT.Copy).then_inc(s_th, 1)
                for t in range(SLOTS):
                    n = t - 2
                    if 0 <= n < NU:
                        act.wait_ge(s_arg, U + n + 1)
                        act.activation(e_t[:, n % 3, lo[n]:], banks[4 + n % 3][:, lo[n]:], ACT.Exp).then_inc(s_ex, 1)
                        act.wait_ge(s_ex, U + n + 1)
                        if n >= 2:
                            act.wait_ge(s_pv, U + n - 1)
                        act.activation(pah[:, n % 2, lo[n]:], e_t[:, n % 3, lo[n]:], ACT.Copy).then_inc(s_ah, 1)
                    n = t
                    if n < NU:
                        if n >= 3:
                            act.wait_ge(s_al, U + n - 2)
                        else:
                            act.wait_ge(s_tl, 4 * i + 4)
                        act.wait_ge(s_z, U + n + 1)
                        e = e_t[:, n % 3, lo[n]:]
                        act.activation(e, banks[4 + n % 3][:, lo[n]:], ACT.Abs).then_inc(s_a1, 1)
                        act.wait_ge(s_a1, 3 * (U + n) + 1)
                        act.activation(e, e, ACT.Exp, scale=-1.0).then_inc(s_a1, 1)
                        act.wait_ge(s_a1, 3 * (U + n) + 2)
                        act.activation(e, e, ACT.Ln, bias=1.0).then_inc(s_a1, 1)
                    if t in (2, 3, 4, 6):
                        gate_step(0, (2, 3, 4, 6).index(t))
                    if t in (14, 15, 16, 18):
                        gate_step(1, (14, 15, 16, 18).index(t))
                    due(tiles_by(t - 1, 2), tiles_by(t, 2))

            with act.Fori(0, NPAIR - 1) as i:
                sb_act(i, N0 + 4 * i)
            sb_act(NPAIR - 1, N0 + 4 * (NPAIR - 1))

            act.wait_ge(s_lo, 2)
            act.preload_act_table_set("exp_and_others")
            act.activation(la[0:HD, :], la[0:HD, :], ACT.Tanh).then_inc(s_lo, 1)
            act.preload_act_table_set("natural_log_exp_and_others")
            DEC = float(np.exp(-0.5))

            def rw_act(i, p_):
                def step(sems, *args, **kw):
                    act.activation(*args, **kw).then_inc(sems["act"], 1)

                for h in range(2):
                    r = 2 * i + h

                    def due(stage, k):
                        if p_ is not None:
                            split_upto(act, split_high, panel_lo, p_, rw_tile(h, stage, k - 1), rw_tile(h, stage, k))

                    def pre(who, name):
                        after(act, s_pre, PRE_STEPS, who, name, r)

                    def quad_prev(who, name):
                        pass

                    def go(*args, **kw):
                        step(s_pre, *args, **kw)

                    if p_ is not None and h == 0:
                        split_upto(act, split_high, panel_lo, p_, 0, 0)
                    t = [tt[:, m] for m in range(6)]
                    pre("dve", "c3")
                    pre("pe", "xw")
                    go(t[0], banks[4][:, :], ACT.Abs, bias=pc[:, 3:4])
                    pre("pe", "xa")
                    go(t[3], banks[5][:, :], ACT.Abs, bias=pc[:, 4:5])
                    pre("act", "w1")
                    go(t[0], t[0], ACT.Exp, scale=-1.0)
                    pre("act", "a1")
                    go(t[3], t[3], ACT.Exp, scale=-1.0)
                    pre("act", "w2")
                    go(t[0], t[0], ACT.Ln, bias=1.0)
                    pre("act", "a2")
                    go(t[3], t[3], ACT.Ln, bias=1.0)
                    pre("dve", "ws")
                    go(t[0], t[0], ACT.Exp)
                    pre("dve", "as")
                    go(t[3], t[3], ACT.Exp)
                    pre("dve", "k")
                    go(t[4], rkv[:, 1], ACT.Square, scale=pc[:, 5:6])
                    due("pre", 1)
                    pre("dve", "cp")
                    go(t[2], t[1], ACT.Exp, scale=-DEC)
                    go(t[0], t[0], ACT.Exp, scale=-DEC)
                    pre("act", "P")
                    go(t[1], t[1], ACT.Exp, scale=DEC)
                    pre("pe", "ss")
                    go(t[4], banks[6][:, :], ACT.Ln, bias=L2_EPS)
                    pre("act", "rn1")
                    go(t[4], t[4], ACT.Exp, scale=-0.5)
                    due("pre", 2)
                    due("pre", 3)

                    for qd in range(2):
                        n = 2 * r + qd

                        def quad(who, name):
                            after(act, s_quad, QUAD_STEPS, who, name, n)

                        def goq(*args, **kw):
                            step(s_quad, *args, **kw)

                        quad("pe", "tr1")
                        goq(tok[:, 0:2], banks[6][:, :], ACT.Copy)
                        quad("pe", "tr2")
                        goq(tok[:, 2:4], banks[7][:, :], ACT.Copy)
                        quad("pe", "x")
                        goq(x_t[:, :, :], banks[6][:, 0:4 * HD], ACT.Copy)
                        for l in range(LV):
                            quad("pe", f"z{l}")
                            goq(z_t[:, :, :], banks[4][:, :], ACT.Copy)
                            due(qd, 2 * l + 1)
                            due(qd, 2 * l + 2)
                        quad("pe", "wt")
                        goq(wt[:, :, :], banks[7][:, 0:2 * P], ACT.Copy, scale=-1.0)
                        quad("pe", "uu")
                        goq(up[:, :, :], banks[6][:, 0:4 * HD], ACT.Copy, scale=-1.0)
                        quad("pe", "y")
                        goq(yb[:, qd * 2 * P:(qd + 1) * 2 * P], banks[7][:, 0:2 * P], ACT.Copy)

                    def post(who, name):
                        after(act, s_post, POST_STEPS, who, name, r)

                    def gop(*args, **kw):
                        step(s_post, *args, **kw)

                    g, gs = ld[:, 0, 0:HALF], ld[:, 1, 0:HALF]
                    act.wait_ge(s_rg, 16 * (r + 1))
                    gop(gs, g, ACT.Abs)
                    post("act", "g1")
                    gop(gs, gs, ACT.Exp, scale=-1.0)
                    post("act", "g2")
                    gop(gs, gs, ACT.Ln, bias=1.0)
                    post("dve", "gm")
                    gop(gs, gs, ACT.Exp)
                    post("dve", "yc")
                    gop(t[4], yb[:, :], ACT.Square)
                    post("pe", "vv")
                    gop(t[4], banks[5][:, :], ACT.Ln, bias=LNX_EPS, scale=1.0 / HD)
                    post("act", "l")
                    gop(t[4], t[4], ACT.Exp, scale=-0.5)

            with act.Fori(0, NPAIR - 1) as i:
                rw_act(i, RW0 + 4 * i)
            rw_act(NPAIR - 1, None)

            with act.Fori(0, 2) as h:
                def chunk_high(c):
                    act.wait_ge(s_v[c % 4], 16 * (h * (NC // 4) + c // 4 + 1))
                    act.wait_ge(s_vused, h * NC + c + 1)
                    act.activation(vh[:, c % 2], v_raw[:, c % 4], ACT.Copy).then_inc(s_vh, 1)

                def panel(n):
                    where, which, m = (rows, 0, n) if n < 4 else (ple, 1, n - 4)
                    act.wait_ge(s_vused, h * NC + LAST[n] + 1 + 2)
                    for b in range(2):
                        act.activation(where[:, b, m * HALF:(m + 1) * HALF], banks[4 * (n % 2) + b][:, :],
                                       ACT.Copy).then_inc(s_ev01, 1)
                    for b in range(HB):
                        act.wait_ge(s_ev01 if b < 2 else s_ev23, 2 * (h * NP_ + n) + b % 2 + 1 + 4)
                        act.wait_ge(s_ss, h * 32 + 4 * n + b + 1)
                        act.activation(sq_out[:, :], where[:, b, m * HALF:(m + 1) * HALF], ACT.Square,
                                       accum_out=ss[:, which, b, m:m + 1]).then_inc(s_ss, 1)

                def inverse_rms(which):
                    act.wait_ge(s_sum, h * 2 + which + 1)
                    act.activation(rs[:, which], rs[:, which], ACT.Ln, bias=RMS_EPS, scale=1.0 / D).then_inc(s_rln, 1)
                    act.wait_ge(s_rln, h * 2 + which + 1)
                    act.activation(rs[:, which], rs[:, which], ACT.Exp, scale=-0.5).then_inc(s_rs, 1)

                def gate(n):
                    for b in range(HB):
                        act.wait_ge(s_vused, h * NC + LAST[n] + 1 + 2)
                        act.wait_ge(s_out, h * 16 + 4 * (n - 8) + b + 1)
                        act.activation(sg[b], banks[4 * (n % 2) + b][:, :], ACT.Exp,
                                       scale=-1.0).then_inc(s_ev01 if b < 2 else s_ev23, 1)

                for m in range(KT // 2):
                    act.wait_ge(s_m[m % 2], 16 * (h * (KT // 4) + m // 2 + 1))
                    act.activation(ah[:, 2 * m:2 * m + 2, :], m_in[:, m % 2], ACT.Copy).then_inc(s_mh, 1)
                    if m < 2:
                        chunk_high(m)
                for k in range(PLE // P):
                    act.wait_ge(s_pt, h * 2 + k + 1)
                    act.activation(ph[:, k], banks[k][:, :], ACT.Copy).then_inc(s_ph, 1)
                for c in range(2, NC):
                    chunk_high(c)
                    if c - 2 in LAST:
                        n = LAST.index(c - 2)
                        panel(n) if n < 8 else gate(n)
                        if n == 3:
                            inverse_rms(0)
                        if n == 7:
                            inverse_rms(1)
                            for k in range(KT):
                                act.wait_ge(s_ht, h * KT + k + 1)
                                act.activation(ah[:, k], banks[k % 4][:, :], ACT.Copy).then_inc(s_hh, 1)
                gate(11)

        @block.vector
        def _(dve):
            for h in range(2):
                for b in range(HB):
                    n = h * HB + b
                    dve.wait_ge(s_rstd, n + 1)
                    dve.tensor_scalar(x_in[:, b], x_in[:, b], rstd[:, n:n + 1], None, ALU.mult).then_inc(s_xn, 1)
                for k in range(KT):
                    dve.wait_ge(s_xh, h * KT + k + 1)
                    dve.scalar_tensor_tensor(out=xl[:, k, h * HALF:(h + 1) * HALF], in0=banks[k % 4][:, :],
                                             scalar=vec("g_pre", k),
                                             in1=xh[:, k, h * HALF:(h + 1) * HALF].bitcast(F32),
                                             op0=ALU.mult, op1=ALU.subtract).then_inc(s_xl, 1)

            for p_ in range(N0):
                for q in range(4):
                    split_low(dve, p_, q)
                    if q == 1 and p_:
                        panel_hi(dve, p_ - 1, (p_ - 1) % 2)
            panel_hi(dve, N0 - 1, 0)

            def sb_dve(i, p_):
                U, due = NU * i, lambda a, b: split_upto(dve, split_low, panel_hi, p_, a, b)
                nd, na = n_diag[-1] * i, n_add[-1] * i

                due(0, 0)
                due(0, PRE)
                dve.wait_ge(s_th, 4 * i + 1)
                dve.scalar_tensor_tensor(out=ql[:, :], in0=raw_q[:, :, :].rearrange("p a n -> p (a n)"), scalar=HD ** -0.5,
                                         in1=qh[:, :].bitcast(F32), op0=ALU.mult, op1=ALU.subtract).then_inc(s_tl, 1)
                dve.wait_ge(s_th, 4 * i + 2)
                dve.tensor_tensor(kl[:, :], raw_k, kh[:, :].bitcast(F32), ALU.subtract).then_inc(s_tl, 1)
                for m in range(2):
                    dve.wait_ge(s_th, 4 * i + 3 + m)
                    dve.tensor_tensor(vtl[:, 4 * m:4 * m + 4, :], banks[4 + m][:, :].rearrange("p (a n) -> p a n", n=P),
                                      vth[:, 4 * m:4 * m + 4, :].bitcast(F32), ALU.subtract).then_inc(s_tl, 1)
                for t in range(SLOTS):
                    n = t - 4
                    if 0 <= n < NU and last[n]:
                        Q, e, _ = UNITS[n]
                        dve.wait_ge(s_pv, U + n + 1)
                        dve.wait_ge(s_gp, 2 * i + Q + 1)
                        h_ = slice(e * HD, e * HD + HD)
                        dve.tensor_tensor(raw_q[h_, 1], banks[7][h_, :], raw_q[h_, 1], ALU.mult).then_inc(s_y, 1)
                    n = t - 2
                    if 0 <= n < NU:
                        dve.wait_ge(s_ah, U + n + 1)
                        dve.tensor_tensor(pal[:, n % 2, lo[n]:], e_t[:, n % 3, lo[n]:], pah[:, n % 2, lo[n]:].bitcast(F32),
                                          ALU.subtract).then_inc(s_al, 1)
                    n = t
                    if n < NU:
                        r, a = r_t[:, n % 2], lo[n]
                        dve.wait_ge(s_a1, 3 * (U + n) + 3)
                        dve.scalar_tensor_tensor(out=r[:, a:], in0=banks[4 + n % 3][:, a:], scalar=0.0,
                                                 in1=e_t[:, n % 3, a:], op0=ALU.max, op1=ALU.add).then_inc(s_sp, 1)
                        dve.wait_ge(s_sp, U + n + 1)
                        if diag[n]:
                            dve.tensor_tensor(r[:, a:a + P], r[:, a:a + P], c_raw[:, 3], ALU.mult).then_inc(s_dm, 1)
                        if not first[n]:
                            dve.tensor_tensor(r[:, lo2[n]:], r[:, lo2[n]:], r_t[:, (n - 1) % 2, lo2[n]:],
                                              ALU.add).then_inc(s_r, 1)
                            dve.wait_ge(s_r, na + n_add[n])
                        if diag[n]:
                            dve.wait_ge(s_dm, nd + n_diag[n])
                        if n >= 2:
                            dve.wait_ge(s_arg, U + n - 1)
                        dve.tensor_copy(rh[:, n % 3, a:], r[:, a:]).then_inc(s_rh, 1)
                        dve.wait_ge(s_rh, U + n + 1)
                        dve.tensor_tensor(rl[:, n % 3, a:], r[:, a:], rh[:, n % 3, a:].bitcast(F32),
                                          ALU.subtract).then_inc(s_rl, 1)
                    if t in (5, 17):
                        Q = (5, 17).index(t)
                        dve.wait_ge(s_ga, 8 * i + 4 * Q + 3)
                        dve.scalar_tensor_tensor(out=raw_q[:, 1], in0=raw_q[:, 0], scalar=0.0, in1=raw_q[:, 1],
                                                 op0=ALU.min, op1=ALU.subtract).then_inc(s_gd, 1)
                    due(tiles_by(t - 1, 2), tiles_by(t, 2))

            with dve.Fori(0, NPAIR - 1) as i:
                sb_dve(i, N0 + 4 * i)
            sb_dve(NPAIR - 1, N0 + 4 * (NPAIR - 1))

            dve.wait_ge(s_la, 16)
            dve.tensor_tensor(la_d[:, 1:S], raw_la[:, 0:S - 1], raw_la[:, 1:S], ALU.subtract).then_inc(s_lo1, 1)
            dve.tensor_scalar(la_d[:, 0:1], raw_la[:, 0:1], -1.0, None, ALU.mult).then_inc(s_lo1, 1)
            dve.wait_ge(s_lo1, 2)
            dve.scalar_tensor_tensor(out=la[:, :], in0=la_d[:, :], scalar=vec("mu", 3 * NPAIR), in1=raw_la[:, 0:S],
                                     op0=ALU.mult, op1=ALU.add).then_inc(s_lo, 2)

            def rw_dve(i, p_):
                for h in range(2):
                    r = 2 * i + h

                    def due(stage, k):
                        if p_ is not None:
                            split_upto(dve, split_low, panel_hi, p_, rw_tile(h, stage, k - 1), rw_tile(h, stage, k))

                    def pre(who, name):
                        after(dve, s_pre, PRE_STEPS, who, name, r)

                    def did(op):
                        op.then_inc(s_pre["dve"], 1)

                    if p_ is not None and h == 0:
                        split_upto(dve, split_low, panel_hi, p_, 0, 0)
                    t = [tt[:, m] for m in range(6)]
                    R, K, V = rkv[:, 0], rkv[:, 1], rkv[:, 2]
                    pcol = lambda m: pc[:, m:m + 1]
                    mu_v = vec_cols[:, vec_at["mu"]:vec_at["mu"] + 3 * NPAIR].rearrange("p (n b) -> p n b", b=NPAIR)
                    co_v = vec_cols[:, vec_at["w0"]:vec_at["w0"] + 7 * NPAIR].rearrange("p (n b) -> p n b", b=NPAIR)
                    did(dve.tensor_copy(pc[:, 0:3], mu_v[:, :, bass.ds(i, 1)].rearrange("p n b -> p (n b)")))
                    did(dve.tensor_copy(pc[:, 3:10], co_v[:, :, bass.ds(i, 1)].rearrange("p n b -> p (n b)")))
                    pre("dve", "c2")
                    did(dve.tensor_scalar(pc[:, 10:11], pc[:, 6:7], -1.0, 1.0, ALU.mult, ALU.add))
                    did(dve.memset(st[:, 0, :] if h == 0 else pc[:, 11:12], 0.0))
                    dve.wait_ge(s_rld, 48 * (r + 1))
                    if h == 0:
                        dve.wait_ge(s_z0, i + 1)
                    did(dve.tensor_tensor(rkv[:, :, :], ld[:, :, 3:3 + HALF], ld[:, :, 4:4 + HALF], ALU.subtract))
                    pre("dve", "d")
                    for m in range(3):
                        did(dve.scalar_tensor_tensor(out=rkv[:, m], in0=rkv[:, m], scalar=pcol(m), in1=ld[:, m, 4:4 + HALF],
                                                     op0=ALU.mult, op1=ALU.add))
                    pre("act", "w1")
                    did(dve.tensor_scalar(t[2], banks[4][:, :], pcol(3), 0.0, ALU.add, ALU.min))
                    pre("dve", "wm")
                    pre("act", "w3")
                    did(dve.tensor_tensor(t[0], t[2], t[0], ALU.subtract))
                    pre("act", "a1")
                    did(dve.tensor_scalar(t[5], banks[5][:, :], pcol(4), 0.0, ALU.add, ALU.min))
                    pre("dve", "am")
                    pre("act", "a3")
                    did(dve.tensor_tensor(t[3], t[5], t[3], ALU.subtract))
                    due("pre", 1)
                    pre("act", "w4")
                    for c in range(HALF // CH):
                        op = dve.tensor_tensor_scan(t[1][:, c * CH:(c + 1) * CH], t[0][:, c * CH:(c + 1) * CH], zero_r[:, :],
                                                    0.0, ALU.add, ALU.add)
                    did(op)
                    pre("dve", "scan")
                    did(dve.tensor_tensor(t[0], t[1], t[0], ALU.subtract))
                    pre("act", "rn2")
                    did(dve.scalar_tensor_tensor(out=t[4], in0=K, scalar=pcol(5), in1=t[4], op0=ALU.mult, op1=ALU.mult))
                    pre("act", "Pp")
                    pre("dve", "kkn")
                    did(dve.tensor_tensor(t[0], t[4], t[0], ALU.mult))
                    pre("act", "a4")
                    did(dve.tensor_tensor(t[4], t[3], t[4], ALU.mult))
                    pre("act", "Pi")
                    pre("dve", "akk")
                    did(dve.tensor_tensor(t[4], t[4], t[1], ALU.mult))
                    did(dve.tensor_scalar(t[3], t[3], pcol(6), pcol(10), ALU.mult, ALU.add))
                    pre("dve", "kt")
                    did(dve.tensor_tensor(K, K, t[3], ALU.mult))
                    pre("dve", "k2")
                    did(dve.scalar_tensor_tensor(out=t[3], in0=R, scalar=pcol(7), in1=K, op0=ALU.mult, op1=ALU.mult))
                    did(dve.tensor_tensor(K, K, t[1], ALU.mult))
                    pre("act", "P")
                    did(dve.tensor_tensor(R, R, t[2], ALU.mult))
                    PC = t[2].rearrange("p (c t) -> p c t", t=CH)[:, :, CH - 1:CH].broadcast_to((P, HALF // CH, CH))
                    pre("dve", "Kh")
                    v3 = lambda a: a.rearrange("p (c t) -> p c t", t=CH)
                    did(dve.tensor_tensor(v3(t[1]), v3(K), PC, ALU.mult))
                    did(dve.tensor_tensor(v3(t[5]), v3(t[4]), PC, ALU.mult))
                    due("pre", 2)
                    pre("pe", "bs")
                    did(dve.tensor_tensor(t[3], banks[7][:, :], V, ALU.mult))
                    due("pre", 3)

                    for qd in range(2):
                        n = 2 * r + qd

                        def quad(who, name):
                            after(dve, s_quad, QUAD_STEPS, who, name, n)

                        def didq(op):
                            op.then_inc(s_quad["dve"], 1)

                        def mask(m):
                            return m_r[:, m:m + 1].broadcast_to((P, 4, P))

                        b4 = [ps[:, 4 + m // 2 * 2:6 + m // 2 * 2, m % 2 * 2 * P:(m % 2 + 1) * 2 * P].rearrange(
                            "p e (b t) -> p e b t", t=P) for m in range(4)]
                        b5 = banks[5][:, :].rearrange("p (u t) -> p u t", t=P)
                        by_head = lambda x: x[:, :, :].rearrange("p (e b) t -> p e b t", e=2)
                        mask4 = lambda m: m_r[:, m:m + 1].rearrange("p (a o) t -> p a o t", o=1).broadcast_to((P, 2, 2, P))
                        dve.wait_ge(s_msk, K_MASK)
                        quad("pe", "gB")
                        didq(dve.tensor_tensor(by_head(n_t), b4[0], mask4(M_STRICT), ALU.mult))
                        quad("dve", "N")
                        didq(dve.tensor_tensor(u_i[:, :, :], n_t[:, :, :], mask(M_PAIR), ALU.mult))
                        quad("dve", "n1")
                        didq(dve.tensor_tensor(u_i[:, :, :], ident[:, :].rearrange("p (o t) -> p o t", o=1).broadcast_to((P, 4, P)), u_i[:, :, :],
                                               ALU.subtract))
                        quad("dve", "u")
                        didq(dve.transpose(t_i[:, :, :].rearrange("p u t -> p (u t)"), u_i[:, :, :].rearrange("p u t -> p (u t)")))
                        for m, (dst, mk) in enumerate(((arb, M_FULL), (aak, M_STRICT), (ark, M_FULL))):
                            quad("pe", ("gB", "gK", "gK")[m])
                            didq(dve.tensor_tensor(by_head(dst), b4[m + 1], mask4(mk), ALU.mult))
                        for l in range(LV):
                            quad("pe", f"v{l}")
                            didq(dve.tensor_tensor(u_i[:, :, :], u_i[:, :, :], b5, ALU.subtract))
                            if l < LV - 1:
                                quad("dve", f"u{l}")
                                didq(dve.transpose(t_i[:, :, :].rearrange("p u t -> p (u t)"),
                                                   u_i[:, :, :].rearrange("p u t -> p (u t)")))
                            due(qd, 2 * l + 1)
                            due(qd, 2 * l + 2)
                        for c in range(4):
                            rows_ = slice(CH * (c % 2), CH * (c % 2) + CH)
                            quad("act", "uc")
                            quad("pe", f"sa{c}")
                            didq(dve.tensor_tensor(sa[rows_, c // 2], banks[4][rows_, 0:P], up[rows_, c // 2], ALU.add))
                            quad("pe", f"st{c}")
                            tk = qd * 4 * CH + c * CH + CH - 1
                            for e in range(2):
                                h_ = slice(e * HD, e * HD + HD)
                                op = dve.scalar_tensor_tensor(out=st[h_, (c + 1) % 2, h_], in0=st[h_, c % 2, h_], scalar=t[2][h_, tk:tk + 1],
                                                              in1=banks[6][h_, h_], op0=ALU.mult, op1=ALU.add)
                            didq(op)

                    def post(who, name):
                        after(dve, s_post, POST_STEPS, who, name, r)

                    def didp(op):
                        op.then_inc(s_post["dve"], 1)

                    g, gs = ld[:, 0, 0:HALF], ld[:, 1, 0:HALF]
                    post("act", "g3")
                    didp(dve.scalar_tensor_tensor(out=gs, in0=g, scalar=0.0, in1=gs, op0=ALU.min, op1=ALU.subtract))
                    post("act", "g4")
                    didp(dve.tensor_tensor(gs, g, gs, ALU.mult))
                    post("pe", "m")
                    didp(dve.scalar_tensor_tensor(out=yb[:, :], in0=banks[4][:, :], scalar=-1.0 / HD, in1=yb[:, :],
                                                  op0=ALU.mult, op1=ALU.add))
                    post("act", "e")
                    didp(dve.tensor_tensor(yb[:, :], yb[:, :], t[4], ALU.mult))
                    post("dve", "yn")
                    didp(dve.tensor_scalar(yb[:, :], yb[:, :], pcol(8), pcol(9), ALU.mult, ALU.add))
                    post("dve", "yw")
                    didp(dve.tensor_tensor(yb[:, :], yb[:, :], t[3], ALU.add))
                    post("dve", "yb")
                    didp(dve.tensor_tensor(yb[:, :], yb[:, :], gs, ALU.mult))

            with dve.Fori(0, NPAIR - 1) as i:
                rw_dve(i, RW0 + 4 * i)
            rw_dve(NPAIR - 1, None)

            for s_, credit in ((s_ml, 2), (s_vl, 4), (s_h, 1), (s_pl, 1), (s_out, 4), (s_ev01, 4), (s_ev23, 4), (s_ss, 1)):
                dve.nop().then_inc(s_, credit)
            dve.wait_ge(s_gb, 32)
            with dve.Fori(0, 2) as h:
                def chunk_low(c):
                    dve.wait_ge(s_vh, h * NC + c + 1)
                    dve.tensor_tensor(vl[:, c % 2], v_raw[:, c % 4], vh[:, c % 2].bitcast(F32),
                                      ALU.subtract).then_inc(s_vl, 1)

                def panel(n):
                    where, m = (rows, n) if n < 4 else (ple, n - 4)
                    dve.wait_ge(s_vused, h * NC + LAST[n] + 1 + 2)
                    for b in range(2, HB):
                        dve.tensor_copy(where[:, b, m * HALF:(m + 1) * HALF],
                                        banks[4 * (n % 2) + b][:, :]).then_inc(s_ev23, 1)

                def sum_squares(which):
                    dve.wait_ge(s_ss, h * 32 + 16 * (which + 1) + 1)
                    dve.tensor_reduce(rs[:, which], ss[:, which], AX_X, ALU.add).then_inc(s_sum, 1)

                def residual(b):
                    dve.wait_ge(s_rs, 2 * h + 1)
                    dve.scalar_tensor_tensor(out=rows[:, b], in0=rows[:, b], scalar=rs[:, 0, b:b + 1], in1=g_post_b[:, :],
                                             op0=ALU.mult, op1=ALU.mult).then_inc(s_gain, 1)
                    dve.wait_ge(s_gain, 8 * h + b + 1)
                    dve.wait_ge(s_xr, 16 * (h * HB + b + 1))
                    dve.tensor_tensor(rows[:, b], rows[:, b], x_res[:, :], ALU.add).then_inc(s_h, 1)

                def gate(n):
                    cols = slice((n - 8) * HALF, (n - 7) * HALF)
                    done = h * 48 + 12 * (n - 8)
                    for b in range(HB):
                        dve.wait_ge(s_ev01 if b < 2 else s_ev23, 2 * (h * NP_ + n) + b % 2 + 1 + 4)
                        dve.tensor_scalar(sg[b], sg[b], 1.0, None, ALU.add).then_inc(s_sgd, 1)
                    for b in range(HB):
                        dve.wait_ge(s_sgd, done + b + 1)
                        dve.reciprocal(sg[b], sg[b]).then_inc(s_sgd, 1)
                    for b in range(HB):
                        dve.wait_ge(s_sgd, done + 4 + b + 1)
                        dve.tensor_tensor(sg[b], sg[b], ple[:, b, cols], ALU.mult).then_inc(s_sgd, 1)
                    for b in range(HB):
                        dve.wait_ge(s_sgd, done + 8 + b + 1)
                        dve.tensor_tensor(rows[:, b, cols], rows[:, b, cols], sg[b], ALU.add).then_inc(s_out, 1)

                for m in range(KT // 2):
                    dve.wait_ge(s_mh, h * (KT // 2) + m + 1)
                    dve.tensor_tensor(al[:, 2 * m:2 * m + 2, :], m_in[:, m % 2], ah[:, 2 * m:2 * m + 2, :].bitcast(F32),
                                      ALU.subtract).then_inc(s_ml, 1)
                    if m < 2:
                        chunk_low(m)
                for k in range(PLE // P):
                    dve.wait_ge(s_ph, h * 2 + k + 1)
                    dve.tensor_tensor(pl[:, k], banks[k][:, :], ph[:, k].bitcast(F32), ALU.subtract).then_inc(s_pl, 1)
                for c in range(2, NC):
                    chunk_low(c)
                    if c - 2 in LAST:
                        n = LAST.index(c - 2)
                        panel(n) if n < 8 else gate(n)
                        if n == 3:
                            sum_squares(0)
                        if 3 <= n < 7:
                            residual(n - 3)
                        if n == 7:
                            sum_squares(1)
                            for k in range(KT):
                                dve.wait_ge(s_hh, h * KT + k + 1)
                                dve.tensor_tensor(al[:, k], banks[k % 4][:, :], ah[:, k].bitcast(F32),
                                                  ALU.subtract).then_inc(s_hl, 1)
                            for b in range(HB):
                                dve.wait_ge(s_rs, 2 * h + 2)
                                dve.scalar_tensor_tensor(out=ple[:, b], in0=ple[:, b], scalar=rs[:, 1, b:b + 1],
                                                         in1=g_ple_b[:, :], op0=ALU.mult, op1=ALU.mult).then_inc(s_gain, 1)
                            dve.wait_ge(s_gain, 8 * h + 8)
                gate(11)

        @block.tensor
        def _(pe):
            pe.wait_ge(s_ident, 1)
            pe.wait_ge(s_vec, 16 * len(vectors))
            pe.transpose(banks[4][:, 0:NVEC], vec_rows[:, :], ident[0:NVEC, 0:NVEC]).then_inc(s_vect, 1)
            for h in range(2):
                pe.wait_ge(s_xn, (h + 1) * HB)
                for k in range(KT):
                    need(pe, s_xl, h * KT + k - 3)
                    for b in range(HB):
                        mm = pe.transpose(banks[k % 4][:, b * P:(b + 1) * P], x_in[:, b, k * P:(k + 1) * P],
                                          ident[:, :])
                    mm.then_inc(s_xt, 1)
            pe.wait_ge(s_xl, 2 * KT)

            for p_ in range(N0):
                for k in range(KT):
                    project_tile(pe, p_, p_ % 2, k)
            pe.wait_ge(s_c2, 2)

            def sb_pe(i, p_):
                U = NU * i
                tiles(pe, p_, 0, PRE // 2)
                pe.wait_ge(s_qkv[2], 16 * (i + 1))
                for m in range(2):
                    for b in range(4):
                        mm = pe.transpose(banks[4 + m][:, b * P:(b + 1) * P],
                                          raw_v[:, (4 * m + b) * P:(4 * m + b + 1) * P], ident[:, :])
                    mm.then_inc(s_vt, 1)
                tiles(pe, p_, PRE // 2, PRE)
                for t in range(SLOTS):
                    n = t
                    if n < NU:
                        Q, e, b = UNITS[n]
                        if n >= 3:
                            pe.wait_ge(s_ex, U + n - 2)
                        elif n == 0:
                            pe.wait_ge(s_tl, 4 * i + 4)
                        h_ = slice(e * HD, e * HD + HD)
                        for m, (kt, qt) in enumerate(((kh, qh), (kh, ql), (kl, qh))):
                            mm = pe.matmul(banks[4 + n % 3][:, lo[n]:], kt[h_, b * P:(b + 1) * P],
                                           qt[h_, Q * HALF + lo[n]:(Q + 1) * HALF], start=(m == 0), stop=(m == 2))
                        mm.then_inc(s_z, 1)
                    tiles(pe, p_, tiles_by(t - 1, 2), tiles_by(t, 0))
                    n = t - 3
                    if 0 <= n < NU:
                        Q, e, b = UNITS[n]
                        if first[n]:
                            need(pe, s_y, 4 * i + chain[n])
                        pe.wait_ge(s_al, U + n + 1)
                        for m, (vt, at) in enumerate(((vth, pah), (vth, pal), (vtl, pah))):
                            mm = pe.matmul(banks[7][:, lo[n]:], vt[:, b], at[:, n % 2, lo[n]:],
                                           start=(first[n] and m == 0), stop=(last[n] and m == 2), skip_group_check=True)
                        mm.then_inc(s_pv, 1)
                    tiles(pe, p_, tiles_by(t, 0), tiles_by(t, 1))
                    n = t - 1
                    if 0 <= n < NU:
                        pe.wait_ge(s_rl, U + n + 1)
                        bank = banks[4 + n % 3]
                        terms = [(c_r[:, 0], rh, n, lo[n]), (c_r[:, 0], rl, n, lo[n])]
                        if not first[n]:
                            terms += [(c_r[:, 1], rh, n - 1, lo2[n]), (c_r[:, 1], rl, n - 1, lo2[n])]
                        if diag[n]:
                            pe.matmul(bank[:, lo[n]:lo[n] + P], c_r[:, 3], c_r[:, 2], start=False, stop=False,
                                      skip_group_check=True)
                        for m, (ct, rt, j, a) in enumerate(terms):
                            mm = pe.matmul(bank[:, a:], ct, rt[:, j % 3, a:], start=False, stop=(m == len(terms) - 1),
                                           skip_group_check=True)
                        mm.then_inc(s_arg, 1)
                    tiles(pe, p_, tiles_by(t, 1), tiles_by(t, 2))

            with pe.Fori(0, NPAIR - 1) as i:
                sb_pe(i, N0 + 4 * i)
            sb_pe(NPAIR - 1, N0 + 4 * (NPAIR - 1))
            def rw_pe(i, p_):
                for h in range(2):
                    r = 2 * i + h

                    def fill(stage, k):
                        if p_ is not None:
                            tiles(pe, p_, rw_tile(h, stage, k - 1), rw_tile(h, stage, k))

                    def pre(who, name):
                        after(pe, s_pre, PRE_STEPS, who, name, r)

                    t = [tt[:, m] for m in range(6)]
                    R, K, V = rkv[:, 0], rkv[:, 1], rkv[:, 2]
                    pe.wait_ge(s_lw, 32 * (i + 1))
                    pe.wait_ge(s_lo, 3)
                    for m in range(2):
                        h_ = slice(m * HD, m * HD + HD)
                        pe.matmul(banks[4 + m][:, :], lw[h_, :], la[h_, h * HALF:(h + 1) * HALF],
                                  start=True, stop=True).then_inc(s_pre["pe"], 1)
                    fill("pre", 1)
                    pre("act", "sq")
                    pe.wait_ge(s_msk, K_MASK)
                    pe.matmul(banks[6][:, :], m_r[:, M_ONES], t[4], start=True, stop=True).then_inc(s_pre["pe"], 1)
                    fill("pre", 2)
                    pre("dve", "rk")
                    pe.matmul(banks[7][:, :], m_r[:, M_ONES], t[3], start=True, stop=True).then_inc(s_pre["pe"], 1)
                    fill("pre", 3)
                    pre("dve", "bon")

                    for qd in range(2):
                        n = 2 * r + qd

                        def quad(who, name, n=n):
                            after(pe, s_quad, QUAD_STEPS, who, name, n)

                        def step(op):
                            op.then_inc(s_quad["pe"], 1)

                        units = [(u, u % 2, u // 2) for u in range(4)]

                        def cols(tl):
                            a = qd * 2 * P + tl * P
                            return slice(a, a + P)

                        if qd:
                            quad("act", "y", n - 1)
                            quad("dve", "st3", n - 1)
                        for m, (lhs, rhs) in enumerate(((t[4], t[0]), (t[4], R), (K, t[0]), (K, R))):
                            for u, tl, e in units:
                                h_ = slice(e * HD, e * HD + HD)
                                a = m % 2 * 2 * P + tl * P
                                mm = pe.matmul(banks[4 + m // 2 * 2 + e][:, a:a + P], lhs[h_, cols(tl)], rhs[h_, cols(tl)],
                                               start=True, stop=True)
                            step(mm)
                        for m, pair in enumerate(((t[0], t[1]), (t[5], V))):
                            quad("dve", "K")
                            for a, src in enumerate(pair):
                                for tl in range(2):
                                    mm = pe.transpose(banks[6 + m][:, (2 * a + tl) * P:(2 * a + tl + 1) * P], src[:, cols(tl)],
                                                      ident[:, :])
                            step(mm)
                        quad("act", "tc2")
                        for u, tl, e in units:
                            mm = pe.matmul(banks[6][:, (2 * tl + e) * HD:(2 * tl + e + 1) * HD], aak[:, u], tok[:, 3, tl, e * HD:(e + 1) * HD],
                                           start=True, stop=True)
                        step(mm)
                        for l in range(LV):
                            quad("pool", f"nb{l}")
                            quad("dve", f"t{l - 1}" if l else "K")
                            for u, _, _ in units:
                                mm = pe.matmul(banks[4][:, u * P:(u + 1) * P], nb[:, l % 2, u], t_i[:, u], start=True, stop=True)
                            step(mm)
                            fill(qd, 2 * l + 1)
                            quad("act", f"z{l}")
                            for u, _, _ in units:
                                mm = pe.matmul(banks[5][:, u * P:(u + 1) * P], z_t[:, u], u_i[:, u], start=True, stop=True)
                            step(mm)
                            fill(qd, 2 * l + 2)
                        quad("dve", f"u{LV - 1}")
                        for u, tl, e in units:
                            mm = pe.matmul(banks[7][e * HD:(e + 1) * HD, tl * P:(tl + 1) * P], tok[:, 0, tl, e * HD:(e + 1) * HD],
                                           u_i[:, u], start=True, stop=True)
                        step(mm)
                        quad("act", "xc")
                        for u, tl, e in units:
                            mm = pe.matmul(banks[6][:, (2 * tl + e) * HD:(2 * tl + e + 1) * HD], u_i[:, u], x_t[:, 2 * tl + e], start=True, stop=True)
                        step(mm)
                        quad("act", "wc")
                        quad("act", "uc")
                        for c in range(4):
                            tl, pp = c // 2, c % 2
                            tr = slice(CH * pp, CH * pp + CH)
                            tc = slice(qd * 2 * P + c * CH, qd * 2 * P + (c + 1) * CH)
                            if c:
                                quad("dve", f"st{c - 1}")
                            step(pe.matmul(banks[4][tr, 0:P], wt[:, tl, tr], st[:, c % 2], start=True, stop=True))
                            if pp == 0:
                                for e in range(2):
                                    pe.matmul(banks[7][e * HD:(e + 1) * HD, tl * P:(tl + 1) * P], tok[:, 3, tl, e * HD:(e + 1) * HD],
                                              ark[:, tl + 2 * e], start=True, stop=False, skip_group_check=True)
                            pe.matmul(banks[7][:, c * CH:(c + 1) * CH], st[:, c % 2], R[:, tc],
                                      start=False, stop=False, skip_group_check=True)
                            pe.matmul(banks[6][:, 0:P], tok[tr, 1, tl], tok[tr, 3, tl], start=True, stop=False)
                            quad("dve", f"sa{c}")
                            step(pe.matmul(banks[6][:, 0:P], tok[tr, 2, tl], sa[tr, tl], start=False, stop=True))
                            if pp == 1:
                                for e in range(2):
                                    mm = pe.matmul(banks[7][e * HD:(e + 1) * HD, tl * P:(tl + 1) * P], sa[:, tl, e * HD:(e + 1) * HD],
                                                   arb[:, tl + 2 * e], start=False, stop=True, skip_group_check=True)
                        step(mm)

                    after(pe, s_quad, QUAD_STEPS, "act", "y", 2 * r + 1)
                    pe.matmul(banks[4][:, :], m_r[:, M_ONES], yb[:, :], start=True, stop=True).then_inc(s_post["pe"], 1)
                    after(pe, s_post, POST_STEPS, "act", "q", r)
                    after(pe, s_quad, QUAD_STEPS, "dve", "st3", 2 * r + 1)
                    pe.matmul(banks[5][:, :], m_r[:, M_ONES], t[4], start=True, stop=True).then_inc(s_post["pe"], 1)
                    after(pe, s_post, POST_STEPS, "dve", "yc", r)
                    after(pe, s_post, POST_STEPS, "act", "l", r)

            with pe.Fori(0, NPAIR - 1) as i:
                rw_pe(i, RW0 + 4 * i)
            rw_pe(NPAIR - 1, None)

            pe.nop().then_inc(s_vused, 2)
            with pe.Fori(0, 2) as h:
                def chunk(c, n, k0, kt, hi, lo):
                    if k0 == 0:
                        pe.wait_ge(s_ev01, 2 * (h * NP_ + n) + 2)
                        pe.wait_ge(s_ev23, 2 * (h * NP_ + n) + 2)
                    pe.wait_ge(s_vl, h * NC + c + 1 + 4)
                    for k2 in range(2):
                        for m, (at, wt) in enumerate(((hi, vh), (hi, vl), (lo, vh))):
                            for b in range(HB):
                                mm = pe.matmul(banks[4 * (n % 2) + b][:, :], at[:, k0 + k2, b * P:(b + 1) * P],
                                               wt[:, c % 2, k2], start=(k0 + k2 == 0 and m == 0),
                                               stop=(k0 + k2 == kt - 1 and m == 2))
                    mm.then_inc(s_vused, 1)

                pe.wait_ge(s_p, 16 * (h + 1))
                pe.wait_ge(s_ev01, 2 * h * NP_ + 4)
                for k in range(PLE // P):
                    for b in range(HB):
                        mm = pe.transpose(banks[k][:, b * P:(b + 1) * P], p_in[:, b, k * P:(k + 1) * P], ident[:, :])
                    mm.then_inc(s_pt, 1)
                pe.wait_ge(s_pl, h * 2 + 2 + 1)
                for c in range(32):
                    if c < 8:
                        pe.wait_ge(s_ml, h * (KT // 2) + c + 1 + 2)
                    chunk(c, c // 8, c % 8 * 2, KT, ah, al)
                for c in range(32, 36):
                    chunk(c, c - 28, 0, 2, ph, pl)
                pe.wait_ge(s_h, h * HB + HB + 1)
                for k in range(KT):
                    if k == 0:
                        pe.wait_ge(s_ev01, 2 * (h * NP_ + 7) + 4)
                        pe.wait_ge(s_ev23, 2 * (h * NP_ + 7) + 4)
                    if k >= 4:
                        pe.wait_ge(s_hl, h * KT + k - 3)
                    for b in range(HB):
                        mm = pe.transpose(banks[k % 4][:, b * P:(b + 1) * P], rows[:, b, k * P:(k + 1) * P], ident[:, :])
                    mm.then_inc(s_ht, 1)
                pe.wait_ge(s_hl, h * KT + KT)
                for c in range(36, NC):
                    chunk(c, 8 + (c - 36) // 8, (c - 36) % 8 * 2, KT, ah, al)


_INS = ["x", "p", "g_pre", "w_in", "mu_shift", "w0", "w_up", "a0", "a_up", "k_k", "k_a", "r_k",
        "lnx_w", "lnx_b", "w_out", "g_post", "w_ple", "w_plg", "g_ple"]


def kernel(**inputs):
    import concourse.bacc as bacc
    from concourse.bass_utils import run_bass_kernel_spmd

    nc = bacc.Bacc("TRN2", target_bir_lowering=False, num_devices=1)
    arrays, args = {}, []
    for name in _INS:
        a = np.ascontiguousarray(inputs[name])
        arrays[f"in_{name}"] = a
        args.append(nc.dram_tensor(f"in_{name}", a.shape, mybir.dt.from_np(a.dtype), kind="ExternalInput").ap())
    shape = tuple(inputs["x"].shape)
    out = nc.dram_tensor("layer_out", shape, F32, kind="ExternalOutput").ap()
    layer_kernel(nc, *args, out)
    r = run_bass_kernel_spmd(nc, [arrays], core_ids=[0])
    return r.results[0]["layer_out"]
```

```python
from contextlib import ExitStack

import numpy as np

import concourse.bass as bass
from concourse import mybir

F32 = mybir.dt.float32
F32R = mybir.dt.float32r
ALU = mybir.AluOpType
ACT = mybir.ActivationFunctionType
AX_X = mybir.AxisListType.X

P = 128
HD = 64
HALF = 512
RMS_EPS = 1e-6
LNX_EPS = 64e-5
L2_EPS = 1e-12


def layer_kernel(nc, x, p, g_pre, w_in, mu_shift, w0, w_up, a0, a_up, k_k, k_a, r_k,
                 lnx_w, lnx_b, w_out, g_post, w_ple, w_plg, g_ple, out):
    S, D = x.shape[1], x.shape[2]
    W = w0.shape[1]
    IN_W = w_in.shape[2]
    PLE = p.shape[3]
    KT = D // P
    TB = S // P
    NPAIR = W // P
    HB = HALF // P
    CH = 64
    QK = 4
    LORA = 3 * NPAIR
    assert S == 2 * HALF and D == 2 * W and IN_W == (8 * NPAIR + 1) * P

    x_rows = x[0].rearrange("(b p) d -> p b d", p=P)
    out_rows = out[0].rearrange("(b p) d -> p b d", p=P)
    p_rows = p[0, 0].rearrange("(b p) d -> p b d", p=P)
    w_out_t = w_out[0].rearrange("(k p) n -> p k n", p=P)
    w_ple_t = w_ple[0].rearrange("(k p) n -> p k n", p=P)
    w_plg_t = w_plg[0].rearrange("(k p) n -> p k n", p=P)
    NC = 2 * (KT // 2) * (D // HALF) + D // HALF
    w_in_t = w_in[0].rearrange("(k p) n -> p k n", p=P)

    vectors = [("g_pre", g_pre), ("mu", mu_shift), ("w0", w0), ("a0", a0), ("k_k", k_k), ("k_a", k_a),
               ("r_k", r_k), ("lnx_w", lnx_w), ("lnx_b", lnx_b)]
    vec_at, NVEC = {}, 0
    for name, v in vectors:
        vec_at[name] = NVEC
        NVEC += v.shape[1] // P

    u_t = nc.dram_tensor("u_t", (IN_W, S), F32, kind="Internal").ap()
    mix_t = nc.dram_tensor("mix_t", (D, S), F32, kind="Internal").ap()

    mask_d = nc.dram_tensor("mask_d", (P, 9 * P), F32, kind="Internal").ap()

    mix_tt = mix_t.rearrange("(k p) s -> p k s", p=P)
    assert PLE == 2 * P and D == 4 * HALF

    with ExitStack() as ctx:
        def sb(name, shape, dt=F32, c=ctx):
            return c.enter_context(nc.sbuf_tensor(name, shape, dt))

        def sem(name):
            return ctx.enter_context(nc.semaphore(name))

        ps = ctx.enter_context(nc.psum_tensor("ps", [P, 8, HALF], F32))
        banks = [ps[:, i] for i in range(8)]

        ident = sb("ident", [P, P])
        vec_rows = sb("vec_rows", [NVEC, P])
        tick = sb("tick", [P, 3])
        vec_cols = sb("vec_cols", [P, NVEC])

        def vec(name, b):
            return vec_cols[:, vec_at[name] + b:vec_at[name] + b + 1]

        with ExitStack() as c1:
            xh = sb("xh", [P, KT, S], F32R, c1)
            xl = sb("xl", [P, KT, S], F32R, c1)
            with ExitStack() as c0:
                x_in = sb("x_in", [P, TB, D], F32, c0)
                sq_junk = sb("sq_junk", [P, D], F32, c0)
                ms = sb("ms", [P, TB], F32, c0)
                rstd = sb("rstd", [P, TB], F32, c0)
            w_raw = sb("w_raw", [P, 2, QK, P], F32, c1)
            wh = sb("wh", [P, 2, QK, P], F32R, c1)
            wl = sb("wl", [P, 2, QK, P], F32R, c1)
            u_stage = sb("u_stage", [P, 2, HALF], F32, c1)
            with ExitStack() as ca:
                raw_q = sb("raw_q", [P, 2, HALF], F32, ca)
                qh = sb("qh", [P, S], F32R, ca)
                ql = sb("ql", [P, S], F32R, ca)
                kh = sb("kh", [P, S], F32R, ca)
                kl = sb("kl", [P, S], F32R, ca)
                vth = sb("vth", [P, TB, P], F32R, ca)
                vtl = sb("vtl", [P, TB, P], F32R, ca)
                e_t = sb("e_t", [P, 3, HALF], F32, ca)
                r_t = sb("r_t", [P, 2, HALF], F32, ca)
                with ExitStack() as cm:
                    m_new = sb("m_new", [P, 9, P], F32, cm)
                rh = sb("rh", [P, 3, HALF], F32R, ca)
                rl = sb("rl", [P, 3, HALF], F32R, ca)
                pah = sb("pah", [P, 2, HALF], F32R, ca)
                pal = sb("pal", [P, 2, HALF], F32R, ca)
                c_raw = sb("c_raw", [P, 4, P], F32, ca)
                c_r = sb("c_r", [P, 4, P], F32R, ca)
            with ExitStack() as cr:
                la = sb("la", [P, S], F32, cr)
                lw = sb("lw", [P, P], F32, cr)
                pc = sb("pc", [P, 12], F32, cr)
                m_r = sb("m_r", [P, 9, P], F32, cr)
                zero_r = sb("zero_r", [P, CH], F32, cr)
                ld = sb("ld", [P, 3, HALF + 4], F32, cr)
                rkv = sb("rkv", [P, 3, HALF], F32, cr)
                tt = sb("tt", [P, 6, HALF], F32, cr)
                n_t = [ld[:, 1 + g, 0:HALF].rearrange("p (u t) -> p u t", t=P) for g in range(2)]
                nb = sb("nb", [P, 2, 4, P], F32, cr)
                arb = sb("arb", [P, 2, 4, P], F32, cr)
                ark = sb("ark", [P, 2, 4, P], F32, cr)
                z_t = sb("z_t", [P, 2, 4, P], F32, cr)
                aak = z_t
                u_i = sb("u_i", [P, 2, 4, P], F32, cr)
                t_i = sb("t_i", [P, 2, 4, P], F32, cr)
                sa = sb("sa", [P, 4, P], F32, cr)
                st = sb("st", [P, 2, P], F32, cr)
                t1_tok = [tt[:, 4].rearrange("p (a b t) -> p a b t", a=2, t=P),
                          rkv[:, 1].rearrange("p (a b t) -> p a b t", a=2, t=P)]
                t2_tok = [tt[:, 0].rearrange("p (a b t) -> p a b t", a=2, t=P),
                          tt[:, 1].rearrange("p (a b t) -> p a b t", a=2, t=P)]
                x_t = [rkv[:, 2, g * 2 * P:(g + 1) * 2 * P].rearrange("p (u v) -> p u v", v=P) for g in range(2)]
                wt = [t_i[:, g, 0:2] for g in range(2)]
                yb = tt[:, 5]
                gate_r = [nb[:, m].rearrange("p u t -> p (u t)") for m in range(2)]
            raw_k = e_t[:, 0:2].rearrange("p a n -> p (a n)")
            raw_la = ld[:, :, :].rearrange("p a n -> p (a n)")
            la_d = rkv[:, 0:2].rearrange("p a n -> p (a n)")
            raw_v = r_t[:, 0:2].rearrange("p a n -> p (a n)")

        with ExitStack() as c3:
            ah = sb("ah", [P, KT, HALF], F32R, c3)
            al = sb("al", [P, KT, HALF], F32R, c3)
            rows = sb("rows", [P, HB, D], F32, c3)
            ple = sb("ple", [P, HB, D], F32, c3)
            v_raw = sb("v_raw", [P, 4, 2, HALF], F32, c3)
            vh = sb("vh", [P, 2, 2, HALF], F32R, c3)
            vl = sb("vl", [P, 2, 2, HALF], F32R, c3)
            g_post_b = sb("g_post_b", [P, D], F32, c3)
            g_ple_b = sb("g_ple_b", [P, D], F32, c3)
            x_res = sb("x_res", [P, D], F32, c3)
            p_in = sb("p_in", [P, HB, PLE], F32, c3)
            m_in = sb("m_in", [P, 2, 2, HALF], F32, c3)
            ss = sb("ss", [P, 2, HB, 4], F32, c3)
            rs = sb("rs", [P, 2, HB], F32, c3)
            sq_out = sb("sq_out", [P, HALF], F32, c3)
            with ExitStack() as cp:
                ph = sb("ph", [P, PLE // P, HALF], F32R, cp)
                pl = sb("pl", [P, PLE // P, HALF], F32R, cp)
            log_sig = sb("log_sig", [P, HB, HALF], F32, c3)
        NP_ = 12
        LAST = [7, 15, 23, 31, 32, 33, 34, 35, 43, 51, 59, 67]
        sg = [x_res[:, i * HALF:(i + 1) * HALF] for i in range(4)]
        sn = [log_sig[:, i] for i in range(4)]

        s_ident0 = sem("s_ident0")
        s_ident = sem("s_ident")
        s_vec = sem("s_vec")
        s_vect = sem("s_vect")
        s_vcol = sem("s_vcol")
        s_x = [sem(f"s_x{b}") for b in range(TB)]
        s_sq = sem("s_sq")
        s_ln = sem("s_ln")
        s_rstd = sem("s_rstd")
        s_xn = sem("s_xn")
        s_xt = sem("s_xt")
        s_xh = sem("s_xh")
        s_xl = sem("s_xl")
        s_w = [sem(f"s_w{i}") for i in range(2)]
        s_wh = sem("s_wh")
        s_wl = sem("s_wl")
        s_wused = sem("s_wused")
        s_ulo = sem("s_ulo")
        s_uhi = sem("s_uhi")
        s_ust = [sem(f"s_ust{i}") for i in range(2)]

        s_c0 = sem("s_c0")
        s_c1 = sem("s_c1")
        s_c2 = sem("s_c2")
        s_qkv = [sem(f"s_qkv{i}") for i in range(3)]
        s_th = sem("s_th")
        s_tl = sem("s_tl")
        s_vt = sem("s_vt")
        s_z = sem("s_z")
        s_a1 = sem("s_a1")
        s_sp = sem("s_sp")
        s_dm = sem("s_dm")
        s_r = sem("s_r")
        s_rh = sem("s_rh")
        s_rl = sem("s_rl")
        s_arg = sem("s_arg")
        s_ex = sem("s_ex")
        s_ah = sem("s_ah")
        s_al = sem("s_al")
        s_pv = sem("s_pv")
        s_y = sem("s_y")
        s_g = sem("s_g")
        s_ga = sem("s_ga")
        s_gd = sem("s_gd")
        s_gp = sem("s_gp")
        s_mst = sem("s_mst")

        s_la = sem("s_la")
        s_lo1 = sem("s_lo1")
        s_lo = sem("s_lo")
        s_msk = sem("s_msk")
        s_mst_d = sem("s_mst_d")
        s_mld = sem("s_mld")
        s_zr = sem("s_zr")
        s_yfree = sem("s_yfree")
        s_rld = sem("s_rld")
        s_lw = sem("s_lw")
        s_z0 = sem("s_z0")
        s_rg = sem("s_rg")
        s_rst = sem("s_rst")
        s_pre = {e: sem(f"s_pre_{e}") for e in ("act", "dve", "pe")}
        s_quad = {e: sem(f"s_quad_{e}") for e in ("act", "dve", "pe", "pool")}
        s_post = {e: sem(f"s_post_{e}") for e in ("act", "dve", "pe")}

        s_gb = sem("s_gb")
        s_m = [sem(f"s_m{i}") for i in range(2)]
        s_mh = sem("s_mh")
        s_ml = sem("s_ml")
        s_v = [sem(f"s_v{i}") for i in range(4)]
        s_vh = sem("s_vh")
        s_vl = sem("s_vl")
        s_vused = sem("s_vused")
        s_ev01 = sem("s_ev01")
        s_ev23 = sem("s_ev23")
        s_ss = sem("s_ss")
        s_sum = sem("s_sum")
        s_rln = sem("s_rln")
        s_rs = sem("s_rs")
        s_gain = sem("s_gain")
        s_xr = sem("s_xr")
        s_h = sem("s_h")
        s_p = sem("s_p")
        s_pt = sem("s_pt")
        s_ph = sem("s_ph")
        s_pl = sem("s_pl")
        s_ht = sem("s_ht")
        s_hh = sem("s_hh")
        s_hl = sem("s_hl")
        s_sg = sem("s_sg")
        s_sgd = sem("s_sgd")
        s_out = sem("s_out")
        s_store = sem("s_store")
        s_tick = sem("s_tick")

        block = ctx.enter_context(nc.Block())

        def need(eng, s, v):
            if not isinstance(v, int) or v > 0:
                eng.wait_ge(s, v)

        SB_COLS = [4 * NPAIR + 1, 5 * NPAIR + 1, 6 * NPAIR + 1, 7 * NPAIR + 1]
        RW_COLS = [0, NPAIR, 2 * NPAIR, 3 * NPAIR + 1]
        N0 = 5
        NPAN = 8 * NPAIR + 1
        UNITS = [(Q, e, b) for Q in range(2) for e in range(2) for b in range(4 * Q + 3, -1, -1)]
        NU = len(UNITS)
        first = [b == 4 * Q + 3 for Q, e, b in UNITS]
        last = [b == 0 for Q, e, b in UNITS]
        diag = [b >= 4 * Q for Q, e, b in UNITS]
        lo = [P * (b - 4 * Q) if b >= 4 * Q else 0 for Q, e, b in UNITS]
        lo2 = [lo[n] + (P if diag[n] else 0) for n in range(NU)]
        n_diag = [sum(diag[:n + 1]) for n in range(NU)]
        n_add = [sum(not f for f in first[:n + 1]) for n in range(NU)]
        chain = [2 * Q + e for Q, e, b in UNITS]
        PRE_V, PRE, SLOTS = 10, 15, NU + 4

        LV = 5
        PRE_STEPS = {
            "dve": "c1 c2 c3 z d r k v wm ws am as scan cp kkn At akk Bh kt k2 rk Kh Rt Kb Bb bon".split(),
            "act": "w1 a1 w2 a2 w3 a3 w4 a4 sq P Pp Pi rn1 rn2".split(),
            "pe": "xw xa ss bs".split()}
        G2, CHUNKS = range(2), HALF // CH
        QUAD_STEPS = {
            "pe": [f"{w}.{g}" for g in G2 for w in ("gN", "gB")] + [f"{w}.{g}" for w in ("gA", "gK") for g in G2]
                  + [f"{w}.{g}" for w in ("tr1", "tr2", "x") for g in G2]
                  + [f"{w}{l}.{g}" for l in range(LV) for w in "zv" for g in G2] + [f"{w}.{g}" for w in ("wt", "uu") for g in G2]
                  + [f"{w}{c}" for c in range(CHUNKS // 2) for w in ("sa", "st")] + ["y.0"]
                  + [f"{w}{c}" for c in range(CHUNKS // 2, CHUNKS) for w in ("sa", "st")] + ["y.1"],
            "dve": [f"{w}.{g}" for g in G2 for w in ("N", "n1", "u", "B", "t")] + [f"{w}.{g}" for g in G2 for w in "AK"]
                   + [f"{w}{l}.{g}" for l in range(LV) for g in G2 for w in ("ut" if l < LV - 1 else "u")]
                   + [f"{w}{c}" for c in range(CHUNKS) for w in ("sa", "st")],
            "act": [f"{w}.{g}" for w in ("tc1", "tc2", "xc") for g in G2] + [f"{w}{l}.{g}" for l in range(LV) for w in ("zz", "z") for g in G2]
                   + [f"{w}.{g}" for w in ("wc", "uc", "y") for g in G2],
            "pool": [f"nb{l}.{g}" for l in range(LV) for g in G2]}
        POST_STEPS = {"pe": ["m", "vv"], "act": "g1 g2 g3 g4 q l e".split(), "dve": "gm gg yc yn yw yb out".split()}

        def half_blocks(x, l, upper):
            b = 2 << l
            return x.rearrange("p (c h t) -> p c h t", h=2, t=b)[:, :, upper]

        def after(eng, sems, steps, who, name, n):
            eng.wait_ge(sems[who], n * len(steps[who]) + steps[who].index(name) + 1)

        M_STRICT, M_FULL, M_ONES, M_PAIR, M_LEV = 0, 1, 2, 3, 4
        RW0 = N0 + 4 * NPAIR

        def columns(a):
            return (HALF - a) * (1 if HALF - a >= 2 * P else 4)

        work = [sum([3 * columns(lo[n]) for n in (t, t - 3) if 0 <= n < NU]
                    + [2 * columns(lo[n]) + (0 if first[n] else 2 * columns(lo2[n])) + (4 * P if diag[n] else 0)
                       for n in (t - 1,) if 0 <= n < NU]) for t in range(SLOTS)]
        room = [max(1700, max(work) - w) for w in work]

        def tiles_by(t, part):
            if t < 0:
                return PRE
            if t == SLOTS - 1:
                return 64
            return PRE + (64 - PRE) * (3 * sum(room[:t]) + (part + 1) * room[t]) // (3 * sum(room[:-1]))

        def load_quarter(sp, col, p_, q):
            need(sp, s_wl, 4 * p_ + q - 1)
            sp.dma_start(w_raw[:, q % 2], w_in_t[:, q * QK:(q + 1) * QK, bass.ds(col * P, P)]).then_inc(s_w[q % 2], 16)

        def store_panel(sp, col, p_):
            sp.wait_ge(s_ulo, p_ + 1)
            sp.dma_start(u_t[bass.ds(col * P, P), 0:HALF], u_stage[:, 0]).then_inc(s_ust[0], 16)
            sp.wait_ge(s_uhi, p_ + 1)
            sp.dma_start(u_t[bass.ds(col * P, P), HALF:S], u_stage[:, 1]).then_inc(s_ust[1], 16)

        def group_io(sp, cols, p_, before):
            for j in range(16):
                load_quarter(sp, cols[j // 4], p_ + j // 4, j % 4)
                if j % 4 == 2:
                    col = cols[j // 4 - 1] if j >= 4 else before
                    if col is not None:
                        store_panel(sp, col, p_ + j // 4 - 1)

        def split_high(act, p_, q):
            act.wait_ge(s_w[q % 2], 16 * (2 * p_ + q // 2 + 1))
            need(act, s_wused, 4 * p_ + q - 1)
            act.activation(wh[:, q % 2], w_raw[:, q % 2], ACT.Copy).then_inc(s_wh, 1)

        def split_low(dve, p_, q):
            dve.wait_ge(s_wh, 4 * p_ + q + 1)
            dve.tensor_tensor(wl[:, q % 2], w_raw[:, q % 2], wh[:, q % 2].bitcast(F32), ALU.subtract).then_inc(s_wl, 1)

        def panel_lo(act, p_, par):
            act.wait_ge(s_wused, 4 * p_ + 4)
            need(act, s_ust[0], 16 * p_)
            act.activation(u_stage[:, 0], banks[2 * par][:, :], ACT.Copy).then_inc(s_ulo, 1)

        def panel_hi(dve, p_, par):
            dve.wait_ge(s_wused, 4 * p_ + 4)
            need(dve, s_ust[1], 16 * p_)
            dve.tensor_copy(u_stage[:, 1], banks[2 * par + 1][:, :]).then_inc(s_uhi, 1)

        def project_tile(pe, p_, par, k):
            q = k // QK
            if k == 0:
                need(pe, s_ulo, p_ - 1)
                need(pe, s_uhi, p_ - 1)
            if k % QK == 0:
                pe.wait_ge(s_wl, 4 * p_ + q + 1)
            for n, (wt, xt) in enumerate(((wh, xh), (wh, xl), (wl, xh))):
                for t in range(2):
                    mm = pe.matmul(banks[2 * par + t][:, :], wt[:, q % 2, k % QK], xt[:, k, t * HALF:(t + 1) * HALF],
                                   start=(k == 0 and n == 0), stop=(k == KT - 1 and n == 2))
            if k % QK == QK - 1:
                mm.then_inc(s_wused, 1)

        def tiles(pe, p_, a, b):
            for j in range(a, b):
                project_tile(pe, p_ + j // KT, (1 + j // KT) % 2, j % KT)

        FILL = {"pre0": 0, "pre1": 8, "pre2": 14, "pre3": 16, "gram1": 19, "gram2": 20, "tr": 21}
        for l in range(LV):
            FILL[f"z{l}"], FILL[f"v{l}"] = [21, 21, 22, 23, 24][l], [21, 22, 23, 24, 24][l]
        for c in range(CHUNKS):
            FILL[f"c{c}"] = [24, 26, 27, 27, 28, 28, 29, 29][c]
        FILL["m"], FILL["post"] = 30, 32
        POINTS = list(FILL)

        def rw_fill(h, point):
            k = POINTS.index(point)
            return 32 * h + FILL[POINTS[k - 1]], 32 * h + FILL[point]

        def split_upto(eng, split, evac, p_, a, b):
            for j in range(a, b + 1):
                if j % 4 == 0 and (j > a or b == 0) and j // 4 + 1 < 16:
                    for jq in ([0, 1] if j == 0 else [j // 4 + 1]):
                        split(eng, p_ + jq // 4, jq % 4)
                if j % KT == 0 and j > a:
                    evac(eng, p_ + j // KT - 1, (j // KT) % 2)

        @block.sync
        def _(sp):
            for h in range(2):
                for b in range(HB):
                    sp.dma_start(x_in[:, h * HB + b], x_rows[:, h * HB + b]).then_inc(s_x[h * HB + b], 16)
                if h == 0:
                    for name, v in vectors:
                        sp.dma_start(vec_rows[vec_at[name]:vec_at[name] + v.shape[1] // P, :],
                                     v[0].rearrange("(b c) -> b c", c=P)).then_inc(s_vec, 16)
            sp.wait_ge(s_xt, 2 * KT)

            group_io(sp, SB_COLS, 0, None)
            for q in range(4):
                load_quarter(sp, LORA, 4, q)
                if q == 2:
                    store_panel(sp, SB_COLS[3], 3)
            group_io(sp, [c + 1 for c in SB_COLS], N0, LORA)
            with sp.Fori(1, NPAIR - 1) as i:
                group_io(sp, [c + i + 1 for c in SB_COLS], N0 + 4 * i, SB_COLS[3] + i)
            group_io(sp, RW_COLS, N0 + 4 * (NPAIR - 1), SB_COLS[3] + NPAIR - 1)
            with sp.Fori(0, NPAIR - 1) as i:
                group_io(sp, [c + i + 1 for c in RW_COLS], N0 + 4 * NPAIR + 4 * i, RW_COLS[3] + i)
            store_panel(sp, RW_COLS[3] + NPAIR - 1, NPAN - 1)

            for t in range(2):
                sp.wait_ge(s_ust[t], 16 * (8 * NPAIR + 1))

            sp.wait_ge(s_wused, 4 * (8 * NPAIR + 1))
            sp.wait_ge(s_wl, 4 * (8 * NPAIR + 1))
            sp.wait_ge(s_ulo, 8 * NPAIR + 1)
            sp.wait_ge(s_uhi, 8 * NPAIR + 1)
            sp.wait_ge(s_mst, 32 * NPAIR)
            sp.wait_ge(s_rst, 32 * NPAIR)
            with sp.Fori(0, 2) as h:
                sp.wait_ge(s_pl, h * 2 + 1)
                sp.dma_start(p_in[:, :, :], p_rows[:, bass.ds(h * HB, HB), :]).then_inc(s_p, 16)

                def load_chunk(c):
                    if c < 32:
                        src = w_out_t[:, 2 * (c % 8):2 * (c % 8) + 2, c // 8 * HALF:(c // 8 + 1) * HALF]
                    elif c < 36:
                        src = w_ple_t[:, :, (c - 32) * HALF:(c - 31) * HALF]
                    else:
                        n, kk = (c - 36) // 8, (c - 36) % 8
                        src = w_plg_t[:, 2 * kk:2 * kk + 2, n * HALF:(n + 1) * HALF]
                    sp.wait_ge(s_vl, h * NC + c + 1)
                    sp.dma_start(v_raw[:, c % 4], src).then_inc(s_v[c % 4], 16)

                for m in range(KT // 2):
                    sp.wait_ge(s_ml, h * (KT // 2) + m + 1)
                    sp.dma_start(m_in[:, m % 2], mix_tt[:, 2 * m:2 * m + 2, bass.ds(h * HALF, HALF)]).then_inc(s_m[m % 2], 16)
                    load_chunk(m)
                for c in range(KT // 2, NC):
                    load_chunk(c)
                    if c in (30, 35, 36, 37):
                        b = max(c - 34, 0)
                        sp.wait_ge(s_h, h * HB + b + 1)
                        sp.wait_ge(s_out, 16 * h + 4)
                        sp.dma_start(x_res[:, :], x_rows[:, h * HB + b, :]).then_inc(s_xr, 16)

        @block.gpsimd
        def _(pool):
            pool.memset(ident[:, :], 0.0).then_inc(s_ident0, 1)
            pool.wait_ge(s_ident0, 1)
            pool.affine_select(out=ident[:, :], in_=ident[:, :], compare_op=ALU.not_equal, fill=1.0, base=0,
                               pattern=[[-1, P]], channel_multiplier=1).then_inc(s_ident, 1)
            pool.wait_ge(s_xl, 2 * KT)
            TILES = [(-1.0, ALU.is_ge, 1), (-1.0, ALU.is_gt, -1), (-2.0 ** 100, ALU.is_ge, 1), (1.0, ALU.is_gt, -1)]
            for n, (value, _, _) in enumerate(TILES):
                pool.memset(c_raw[:, n], value).then_inc(s_c0, 1)
            for n, (_, op, sign) in enumerate(TILES):
                pool.wait_ge(s_c0, n + 1)
                pool.affine_select(out=c_raw[:, n], in_=c_raw[:, n], compare_op=op, fill=0.0, base=0,
                                   pattern=[[-sign, P]], channel_multiplier=sign).then_inc(s_c1, 1)

            pool.memset(tick[:, :], 0.0).then_inc(s_msk, 1)
            pool.memset(m_new[:, :, :], 1.0).then_inc(s_msk, 1)
            k_ = 2

            def select(tile, pattern, base, cm, op):
                nonlocal k_
                pool.wait_ge(s_msk, k_)
                pool.affine_select(out=tile, in_=tile, compare_op=op, fill=0.0, base=base, pattern=pattern,
                                   channel_multiplier=cm).then_inc(s_msk, 1)
                k_ += 1

            def same_block(tile, width):
                v = tile.rearrange("p (c t) -> p c t", t=width)
                select(v, [[-width, P // width], [0, width]], 0, 1, ALU.is_ge)
                select(v, [[width, P // width], [0, width]], width - 1, -1, ALU.is_ge)

            for m in (M_STRICT, M_FULL, M_ONES):
                same_block(m_new[:, m], CH)
            select(m_new[:, M_STRICT], [[1, P]], 0, -1, ALU.is_gt)
            select(m_new[:, M_FULL], [[1, P]], 0, -1, ALU.is_ge)
            for l in range(LV + 1):
                b = 1 << l
                m = m_new[:, M_PAIR + l]
                same_block(m, 2 * b)
                v = m.rearrange("p (c h t) -> p c h t", h=2, t=b)
                select(v, [[2 * b, P // (2 * b)], [0, 2], [0, b]], b, -1, ALU.is_gt)
                select(v, [[0, P // (2 * b)], [1, 2], [0, b]], 0, 0, ALU.is_gt)

            pool.wait_ge(s_msk, k_)
            pool.dma_start(mask_d[:, :].rearrange("p (m t) -> p m t", t=P), m_new[:, :, :]).then_inc(s_mst_d, 16)

            def sb_io(i):
                rows = D // 2 + i * P
                for t in range(2):
                    pool.wait_ge(s_ust[t], 16 * (N0 + 4 * i))
                for n, dst in enumerate((raw_q[:, :, :].rearrange("p a n -> p (a n)"), raw_k, raw_v)):
                    pool.dma_start(dst, u_t[bass.ds((SB_COLS[n] + i) * P, P), :]).then_inc(s_qkv[n], 16)
                for Q in range(2):
                    if Q == 0:
                        pool.wait_ge(s_tl, 4 * i + 1)
                    else:
                        pool.wait_ge(s_mst, 32 * i + 16)
                    pool.dma_start(raw_q[:, 0], u_t[bass.ds((SB_COLS[3] + i) * P, P), Q * HALF:(Q + 1) * HALF]).then_inc(s_g, 16)
                    pool.wait_ge(s_ga, 8 * i + 4 * Q + 4)
                    pool.tensor_tensor(raw_q[:, 1], raw_q[:, 0], raw_q[:, 1], ALU.mult).then_inc(s_gp, 1)
                    pool.wait_ge(s_y, 4 * i + 2 * Q + 2)
                    pool.dma_start(mix_t[bass.ds(rows, P), Q * HALF:(Q + 1) * HALF], raw_q[:, 1]).then_inc(s_mst, 16)
                pool.wait_ge(s_mst, 32 * i + 32)

            with pool.Fori(0, NPAIR - 1) as i:
                sb_io(i)
            sb_io(NPAIR - 1)

            pool.dma_start(m_r[:, :, :], mask_d[:, :].rearrange("p (m t) -> p m t", t=P)).then_inc(s_mld, 16)
            pool.memset(zero_r[:, :], 0.0).then_inc(s_zr, 1)
            pool.memset(st[:, :, :], 0.0).then_inc(s_zr, 1)
            pool.tensor_tensor(tick[:, 1:2], tick[:, 0:1], tick[:, 0:1], ALU.add).then_inc(s_yfree, 1)
            for t in range(2):
                pool.wait_ge(s_ust[t], 16 * N0)
            pool.dma_start(raw_la[:, 0:S], u_t[LORA * P:LORA * P + P, :]).then_inc(s_la, 16)

            def rw_load(i, h):
                if h == 0:
                    for t in range(2):
                        pool.wait_ge(s_ust[t], 16 * (RW0 + 4 * i - 1))
                    pool.dma_start(lw[0:HD, :], w_up[0][:, bass.ds(i * P, P)]).then_inc(s_lw, 16)
                    pool.dma_start(lw[HD:P, :], a_up[0][:, bass.ds(i * P, P)]).then_inc(s_lw, 16)
                    pool.memset(ld[:, :, 3:4], 0.0).then_inc(s_z0, 1)
                for n in range(3):
                    row = (RW_COLS[n] + i) * P
                    if h == 0:
                        pool.dma_start(ld[:, n, 4:4 + HALF], u_t[bass.ds(row, P), 0:HALF]).then_inc(s_rld, 16)
                    else:
                        pool.dma_start(ld[:, n, 3:4 + HALF], u_t[bass.ds(row, P), HALF - 1:S]).then_inc(s_rld, 16)

            def rw_io(i, more):
                for h in range(2):
                    r = 2 * i + h
                    for l in range(LV):
                        for g in range(2):
                            if l == 0:
                                after(pool, s_quad, QUAD_STEPS, "dve", f"N.{g}", r)
                            else:
                                after(pool, s_quad, QUAD_STEPS, "pe", f"z{l - 1}.{g}", r)
                            pool.tensor_tensor(nb[:, g], n_t[g], m_r[:, M_LEV + l:M_LEV + l + 1].broadcast_to((P, 4, P)),
                                               ALU.mult).then_inc(s_quad["pool"], 1)
                    after(pool, s_quad, QUAD_STEPS, "pool", f"nb{LV - 1}.1", r)
                    if h == 0:
                        rw_load(i, 1)
                    elif more:
                        rw_load(i + 1, 0)
                    for t in range(2):
                        pool.wait_ge(s_ust[t], 16 * (RW0 + 4 * i))
                    after(pool, s_quad, QUAD_STEPS, "pe", f"z{LV - 1}.1", r)
                    pool.dma_start(gate_r[0], u_t[bass.ds((RW_COLS[3] + i) * P, P), h * HALF:(h + 1) * HALF]).then_inc(s_rg, 16)
                    pool.wait_ge(s_yfree, 2 * r + 1)
                    after(pool, s_post, POST_STEPS, "dve", "out", r)
                    pool.tensor_tensor(tick[:, 1:2], tick[:, 0:1], tick[:, 0:1], ALU.add).then_inc(s_yfree, 1)
                    pool.dma_start(mix_t[bass.ds(i * P, P), h * HALF:(h + 1) * HALF], yb).then_inc(s_rst, 16)
                    pool.wait_ge(s_yfree, 2 * r + 2)
                    pool.wait_ge(s_rst, 16 * (r + 1))
                    pool.tensor_tensor(tick[:, 1:2], tick[:, 0:1], tick[:, 0:1], ALU.add).then_inc(s_yfree, 1)

            pool.wait_ge(s_lo, 3)
            rw_load(0, 0)
            pool.wait_ge(s_mld, 16)
            with pool.Fori(0, NPAIR - 1) as i:
                rw_io(i, True)
            rw_io(NPAIR - 1, False)

            pool.wait_ge(s_rst, 32 * NPAIR)
            pool.tensor_tensor(tick[:, 2:3], tick[:, 0:1], tick[:, 0:1], ALU.add).then_inc(s_tick, 1)
            pool.wait_ge(s_vh, KT // 2)
            pool.dma_start(g_post_b[:, :], g_post[0:1, :].broadcast_to((P, D))).then_inc(s_gb, 16)
            pool.dma_start(g_ple_b[:, :], g_ple[0:1, :].broadcast_to((P, D))).then_inc(s_gb, 16)
            with pool.Fori(0, 2) as h:
                for n in range(4):
                    for b in range(HB):
                        pool.wait_ge(s_tick, h * 17 + 4 * n + b + 1)
                        pool.wait_ge(s_out, h * 16 + 4 * n + b + 1 + 4)
                        pool.tensor_tensor(tick[:, 2:3], tick[:, 0:1], tick[:, 0:1], ALU.add).then_inc(s_tick, 1)
                        pool.dma_start(out_rows[:, h * HB + b, n * HALF:(n + 1) * HALF],
                                       rows[:, b, n * HALF:(n + 1) * HALF]).then_inc(s_store, 16)
                pool.wait_ge(s_tick, h * 17 + 17)
                pool.wait_ge(s_store, 256 * h + 256)
                pool.tensor_tensor(tick[:, 2:3], tick[:, 0:1], tick[:, 0:1], ALU.add).then_inc(s_tick, 1)
            pool.wait_ge(s_store, 512)

        @block.scalar
        def _(act):
            act.preload_act_table_set("natural_log_exp_and_others")
            def rms(n):
                act.wait_ge(s_x[n], 16)
                if n:
                    act.wait_ge(s_sq, n)
                act.activation(sq_junk[:, :], x_in[:, n], ACT.Square, accum_out=ms[:, n:n + 1]).then_inc(s_sq, 1)
                act.wait_ge(s_sq, n + 1)
                act.activation(rstd[:, n:n + 1], ms[:, n:n + 1], ACT.Ln, bias=RMS_EPS, scale=1.0 / D).then_inc(s_ln, 1)
                act.wait_ge(s_ln, n + 1)
                act.activation(rstd[:, n:n + 1], rstd[:, n:n + 1], ACT.Exp, scale=-0.5).then_inc(s_rstd, 1)

            for n in range(HB):
                rms(n)
            act.wait_ge(s_vect, 1)
            act.activation(vec_cols[:, :], banks[4][:, 0:NVEC], ACT.Copy).then_inc(s_vcol, 1)
            act.wait_ge(s_vcol, 1)
            for h in range(2):
                for k in range(KT):
                    act.wait_ge(s_xt, h * KT + k + 1)
                    act.activation(xh[:, k, h * HALF:(h + 1) * HALF], banks[k % 4][:, :], ACT.Copy,
                                   scale=vec("g_pre", k)).then_inc(s_xh, 1)
                    if h == 0 and k % 4 == 3:
                        rms(HB + k // 4)

            for p_ in range(N0):
                for q in range(4):
                    split_high(act, p_, q)
                    if q == 1 and p_:
                        panel_lo(act, p_ - 1, (p_ - 1) % 2)
            panel_lo(act, N0 - 1, 0)
            act.wait_ge(s_c1, 4)
            act.activation(c_r[:, 0:3], c_raw[:, 0:3], ACT.Copy).then_inc(s_c2, 1)
            act.activation(c_r[:, 3], ident[:, :], ACT.Copy).then_inc(s_c2, 1)

            def sb_act(i, p_):
                U, due = NU * i, lambda a, b: split_upto(act, split_high, panel_lo, p_, a, b)

                def gate_step(Q, step):
                    done = 8 * i + 4 * Q
                    if step == 0:
                        act.wait_ge(s_g, 16 * (2 * i + Q + 1))
                        act.activation(raw_q[:, 1], raw_q[:, 0], ACT.Abs).then_inc(s_ga, 1)
                    elif step == 1:
                        act.wait_ge(s_ga, done + 1)
                        act.activation(raw_q[:, 1], raw_q[:, 1], ACT.Exp, scale=-1.0).then_inc(s_ga, 1)
                    elif step == 2:
                        act.wait_ge(s_ga, done + 2)
                        act.activation(raw_q[:, 1], raw_q[:, 1], ACT.Ln, bias=1.0).then_inc(s_ga, 1)
                    else:
                        act.wait_ge(s_gd, 2 * i + Q + 1)
                        act.activation(raw_q[:, 1], raw_q[:, 1], ACT.Exp).then_inc(s_ga, 1)

                due(0, 0)
                due(0, PRE)
                act.wait_ge(s_qkv[0], 16 * (i + 1))
                act.activation(qh[:, :], raw_q[:, :, :].rearrange("p a n -> p (a n)"), ACT.Copy, scale=HD ** -0.5).then_inc(s_th, 1)
                act.wait_ge(s_qkv[1], 16 * (i + 1))
                act.activation(kh[:, :], raw_k, ACT.Copy).then_inc(s_th, 1)
                for m in range(2):
                    act.wait_ge(s_vt, 2 * i + m + 1)
                    act.activation(vth[:, 4 * m:4 * m + 4, :], banks[4 + m][:, :], ACT.Copy).then_inc(s_th, 1)
                for t in range(SLOTS):
                    n = t - 2
                    if 0 <= n < NU:
                        act.wait_ge(s_arg, U + n + 1)
                        act.activation(e_t[:, n % 3, lo[n]:], banks[4 + n % 3][:, lo[n]:], ACT.Exp).then_inc(s_ex, 1)
                        act.wait_ge(s_ex, U + n + 1)
                        if n >= 2:
                            act.wait_ge(s_pv, U + n - 1)
                        act.activation(pah[:, n % 2, lo[n]:], e_t[:, n % 3, lo[n]:], ACT.Copy).then_inc(s_ah, 1)
                    n = t
                    if n < NU:
                        if n >= 3:
                            act.wait_ge(s_al, U + n - 2)
                        else:
                            act.wait_ge(s_tl, 4 * i + 4)
                        act.wait_ge(s_z, U + n + 1)
                        e = e_t[:, n % 3, lo[n]:]
                        act.activation(e, banks[4 + n % 3][:, lo[n]:], ACT.Abs).then_inc(s_a1, 1)
                        act.wait_ge(s_a1, 3 * (U + n) + 1)
                        act.activation(e, e, ACT.Exp, scale=-1.0).then_inc(s_a1, 1)
                        act.wait_ge(s_a1, 3 * (U + n) + 2)
                        act.activation(e, e, ACT.Ln, bias=1.0).then_inc(s_a1, 1)
                    if t in (2, 3, 4, 6):
                        gate_step(0, (2, 3, 4, 6).index(t))
                    if t in (14, 15, 16, 18):
                        gate_step(1, (14, 15, 16, 18).index(t))
                    due(tiles_by(t - 1, 2), tiles_by(t, 2))

            with act.Fori(0, NPAIR - 1) as i:
                sb_act(i, N0 + 4 * i)
            sb_act(NPAIR - 1, N0 + 4 * (NPAIR - 1))

            act.wait_ge(s_lo, 2)
            act.wait_ge(s_zr, 2)
            act.preload_act_table_set("exp_and_others")
            act.activation(la[0:HD, :], la[0:HD, :], ACT.Tanh).then_inc(s_lo, 1)
            act.preload_act_table_set("natural_log_exp_and_others")
            DEC = float(np.exp(-0.5))

            def rw_act(i, p_):
                def step(sems, *args, **kw):
                    act.activation(*args, **kw).then_inc(sems["act"], 1)

                for h in range(2):
                    r = 2 * i + h

                    def due(point):
                        if p_ is not None:
                            split_upto(act, split_high, panel_lo, p_, *rw_fill(h, point))

                    def pre(who, name):
                        after(act, s_pre, PRE_STEPS, who, name, r)

                    def go(*args, **kw):
                        step(s_pre, *args, **kw)

                    if p_ is not None and h == 0:
                        split_upto(act, split_high, panel_lo, p_, 0, 0)
                    t = [tt[:, m] for m in range(6)]
                    pre("dve", "c3")
                    pre("pe", "xw")
                    go(t[0], banks[4][:, :], ACT.Abs, bias=pc[:, 3:4])
                    pre("pe", "xa")
                    go(t[3], banks[5][:, :], ACT.Abs, bias=pc[:, 4:5])
                    pre("act", "w1")
                    go(t[0], t[0], ACT.Exp, scale=-1.0)
                    pre("act", "a1")
                    go(t[3], t[3], ACT.Exp, scale=-1.0)
                    pre("act", "w2")
                    go(t[0], t[0], ACT.Ln, bias=1.0)
                    pre("act", "a2")
                    go(t[3], t[3], ACT.Ln, bias=1.0)
                    pre("dve", "ws")
                    go(t[0], t[0], ACT.Exp)
                    pre("dve", "as")
                    go(t[3], t[3], ACT.Exp)
                    pre("dve", "k")
                    go(t[4], rkv[:, 1], ACT.Square, scale=pc[:, 5:6])
                    due("pre1")
                    pre("dve", "cp")
                    go(t[2], t[1], ACT.Exp, scale=-DEC)
                    go(t[0], t[0], ACT.Exp, scale=-DEC)
                    pre("act", "P")
                    go(t[1], t[1], ACT.Exp, scale=DEC)
                    pre("pe", "ss")
                    go(t[4], banks[6][:, :], ACT.Ln, bias=L2_EPS)
                    pre("act", "rn1")
                    go(t[4], t[4], ACT.Exp, scale=-0.5)
                    due("pre2")
                    due("pre3")

                    def quad(who, name):
                        after(act, s_quad, QUAD_STEPS, who, name, r)

                    def goq(*args, **kw):
                        step(s_quad, *args, **kw)

                    flat = lambda x: x.rearrange("p u t -> p (u t)")

                    due("gram1")
                    due("gram2")
                    for m, dst in enumerate((t1_tok, t2_tok)):
                        for g in range(2):
                            quad("pe", f"tr{m + 1}.{g}")
                            goq(dst[g], banks[4 + 2 * g + m][:, :], ACT.Copy)
                    due("tr")
                    for g in range(2):
                        quad("pe", f"x.{g}")
                        goq(x_t[g], banks[4 + 2 * g][:, 0:4 * HD], ACT.Copy)
                    for l in range(LV):
                        for g in range(2):
                            quad("pe", f"v{l - 1}.{g}" if l else f"x.{g}")
                            n = HALF // 2 // (2 << l)
                            goq(half_blocks(flat(z_t[:, g]), l, 1), zero_r[:, 0:2 << l].rearrange("p (o t) -> p o t", o=1).broadcast_to(
                                (P, n, 2 << l)), ACT.Copy)
                        for g in range(2):
                            quad("pe", f"z{l}.{g}")
                            goq(half_blocks(flat(z_t[:, g]), l, 0),
                                banks[4 + 2 * g][:, 0:HALF // 2].rearrange("p (c t) -> p c t", t=2 << l), ACT.Copy)
                        due(f"z{l}")
                        due(f"v{l}")
                    for g in range(2):
                        quad("pe", f"wt.{g}")
                        goq(wt[g], banks[5 + 2 * g][:, 0:2 * P], ACT.Copy, scale=-1.0)
                    for g in range(2):
                        quad("pe", f"uu.{g}")
                        goq(x_t[g], banks[4 + 2 * g][:, 0:4 * HD], ACT.Copy, scale=-1.0)
                    def post(who, name):
                        after(act, s_post, POST_STEPS, who, name, r)

                    def gop(*args, **kw):
                        step(s_post, *args, **kw)

                    g, gs = gate_r
                    act.wait_ge(s_rg, 16 * (r + 1))
                    gop(gs, g, ACT.Abs)
                    post("act", "g1")
                    gop(gs, gs, ACT.Exp, scale=-1.0)
                    post("act", "g2")
                    gop(gs, gs, ACT.Ln, bias=1.0)
                    post("dve", "gm")
                    gop(gs, gs, ACT.Exp)
                    for c in range(CHUNKS):
                        due(f"c{c}")
                    for g in range(2):
                        quad("pe", f"y.{g}")
                        goq(yb[:, g * 2 * P:(g + 1) * 2 * P], banks[5 + 2 * g][:, 0:2 * P], ACT.Copy)

                    due("m")
                    post("dve", "yc")
                    gop(t[4], yb, ACT.Square)
                    post("pe", "vv")
                    gop(t[4], banks[5][:, :], ACT.Ln, bias=LNX_EPS, scale=1.0 / HD)
                    post("act", "l")
                    gop(t[4], t[4], ACT.Exp, scale=-0.5)
                    due("post")

            with act.Fori(0, NPAIR - 1) as i:
                rw_act(i, RW0 + 4 * i)
            rw_act(NPAIR - 1, None)

            with act.Fori(0, 2) as h:
                def chunk_high(c):
                    act.wait_ge(s_v[c % 4], 16 * (h * (NC // 4) + c // 4 + 1))
                    act.wait_ge(s_vused, h * NC + c + 1)
                    act.activation(vh[:, c % 2], v_raw[:, c % 4], ACT.Copy).then_inc(s_vh, 1)

                def panel(n):
                    where, which, m = (rows, 0, n) if n < 4 else (ple, 1, n - 4)
                    act.wait_ge(s_vused, h * NC + LAST[n] + 1 + 2)
                    for b in range(2):
                        act.activation(where[:, b, m * HALF:(m + 1) * HALF], banks[4 * (n % 2) + b][:, :],
                                       ACT.Copy).then_inc(s_ev01, 1)
                    for b in range(HB):
                        act.wait_ge(s_ev01 if b < 2 else s_ev23, 2 * (h * NP_ + n) + b % 2 + 1 + 4)
                        act.wait_ge(s_ss, h * 32 + 4 * n + b + 1)
                        act.activation(sq_out[:, :], where[:, b, m * HALF:(m + 1) * HALF], ACT.Square,
                                       accum_out=ss[:, which, b, m:m + 1]).then_inc(s_ss, 1)

                def inverse_rms(which):
                    act.wait_ge(s_sum, h * 2 + which + 1)
                    act.activation(rs[:, which], rs[:, which], ACT.Ln, bias=RMS_EPS, scale=1.0 / D).then_inc(s_rln, 1)
                    act.wait_ge(s_rln, h * 2 + which + 1)
                    act.activation(rs[:, which], rs[:, which], ACT.Exp, scale=-0.5).then_inc(s_rs, 1)

                def gate(n, step):
                    done = h * 64 + 16 * (n - 8)
                    for b in range(HB):
                        if step == 0:
                            act.wait_ge(s_vused, h * NC + LAST[n] + 1 + 2)
                            act.wait_ge(s_out, h * 16 + 4 * (n - 8) + b + 1)
                            op = act.activation(sg[b], banks[4 * (n % 2) + b][:, :], ACT.Abs)
                        elif step < 3:
                            act.wait_ge(s_sg, done + 4 * (step - 1) + b + 1 + 1)
                            op = (act.activation(sg[b], sg[b], ACT.Exp, scale=-1.0) if step == 1
                                  else act.activation(sg[b], sg[b], ACT.Ln, bias=1.0))
                        else:
                            act.wait_ge(s_sgd, h * 32 + 8 * (n - 8) + b + 1)
                            op = act.activation(sg[b], sn[b], ACT.Exp)
                        op.then_inc(s_sg, 1)

                for k in range(PLE // P):
                    act.wait_ge(s_sg, h * 64 + 1)
                    act.wait_ge(s_pt, h * 2 + k + 1)
                    act.activation(ph[:, k], banks[k][:, :], ACT.Copy).then_inc(s_ph, 1)
                for m in range(KT // 2):
                    act.wait_ge(s_m[m % 2], 16 * (h * (KT // 4) + m // 2 + 1))
                    act.activation(ah[:, 2 * m:2 * m + 2, :], m_in[:, m % 2], ACT.Copy).then_inc(s_mh, 1)
                    chunk_high(m)
                act.wait_ge(s_tick, h * 17 + 1)
                for c in range(KT // 2, NC):
                    chunk_high(c)
                    for step in range(1, 4):
                        if c - 2 - step in LAST[8:]:
                            gate(LAST.index(c - 2 - step), step)
                    if c - 2 in LAST:
                        n = LAST.index(c - 2)
                        panel(n) if n < 8 else gate(n, 0)
                        if n == 3:
                            inverse_rms(0)
                        if n == 7:
                            inverse_rms(1)
                            for k in range(KT):
                                act.wait_ge(s_ht, h * KT + k + 1)
                                act.activation(ah[:, k], banks[k % 4][:, :], ACT.Copy).then_inc(s_hh, 1)
                for step in range(4):
                    gate(11, step)

        @block.vector
        def _(dve):
            def scale(n):
                dve.wait_ge(s_rstd, n + 1)
                dve.tensor_scalar(x_in[:, n], x_in[:, n], rstd[:, n:n + 1], None, ALU.mult).then_inc(s_xn, 1)

            for n in range(HB):
                scale(n)
            for h in range(2):
                for k in range(KT):
                    dve.wait_ge(s_xh, h * KT + k + 1)
                    dve.scalar_tensor_tensor(out=xl[:, k, h * HALF:(h + 1) * HALF], in0=banks[k % 4][:, :],
                                             scalar=vec("g_pre", k),
                                             in1=xh[:, k, h * HALF:(h + 1) * HALF].bitcast(F32),
                                             op0=ALU.mult, op1=ALU.subtract).then_inc(s_xl, 1)
                    if h == 0 and k % 4 == 3:
                        scale(HB + k // 4)

            for p_ in range(N0):
                for q in range(4):
                    split_low(dve, p_, q)
                    if q == 1 and p_:
                        panel_hi(dve, p_ - 1, (p_ - 1) % 2)
            panel_hi(dve, N0 - 1, 0)
            dve.wait_ge(s_mst_d, 16)

            def sb_dve(i, p_):
                U, due = NU * i, lambda a, b: split_upto(dve, split_low, panel_hi, p_, a, b)
                nd, na = n_diag[-1] * i, n_add[-1] * i

                due(0, 0)
                due(0, PRE)
                dve.wait_ge(s_th, 4 * i + 1)
                dve.scalar_tensor_tensor(out=ql[:, :], in0=raw_q[:, :, :].rearrange("p a n -> p (a n)"), scalar=HD ** -0.5,
                                         in1=qh[:, :].bitcast(F32), op0=ALU.mult, op1=ALU.subtract).then_inc(s_tl, 1)
                dve.wait_ge(s_th, 4 * i + 2)
                dve.tensor_tensor(kl[:, :], raw_k, kh[:, :].bitcast(F32), ALU.subtract).then_inc(s_tl, 1)
                for m in range(2):
                    dve.wait_ge(s_th, 4 * i + 3 + m)
                    dve.tensor_tensor(vtl[:, 4 * m:4 * m + 4, :], banks[4 + m][:, :].rearrange("p (a n) -> p a n", n=P),
                                      vth[:, 4 * m:4 * m + 4, :].bitcast(F32), ALU.subtract).then_inc(s_tl, 1)
                for t in range(SLOTS):
                    n = t - 4
                    if 0 <= n < NU and last[n]:
                        Q, e, _ = UNITS[n]
                        dve.wait_ge(s_pv, U + n + 1)
                        dve.wait_ge(s_gp, 2 * i + Q + 1)
                        h_ = slice(e * HD, e * HD + HD)
                        dve.tensor_tensor(raw_q[h_, 1], banks[7][h_, :], raw_q[h_, 1], ALU.mult).then_inc(s_y, 1)
                    n = t - 2
                    if 0 <= n < NU:
                        dve.wait_ge(s_ah, U + n + 1)
                        dve.tensor_tensor(pal[:, n % 2, lo[n]:], e_t[:, n % 3, lo[n]:], pah[:, n % 2, lo[n]:].bitcast(F32),
                                          ALU.subtract).then_inc(s_al, 1)
                    n = t
                    if n < NU:
                        r, a = r_t[:, n % 2], lo[n]
                        dve.wait_ge(s_a1, 3 * (U + n) + 3)
                        dve.scalar_tensor_tensor(out=r[:, a:], in0=banks[4 + n % 3][:, a:], scalar=0.0,
                                                 in1=e_t[:, n % 3, a:], op0=ALU.max, op1=ALU.add).then_inc(s_sp, 1)
                        dve.wait_ge(s_sp, U + n + 1)
                        if diag[n]:
                            dve.tensor_tensor(r[:, a:a + P], r[:, a:a + P], c_raw[:, 3], ALU.mult).then_inc(s_dm, 1)
                        if not first[n]:
                            dve.tensor_tensor(r[:, lo2[n]:], r[:, lo2[n]:], r_t[:, (n - 1) % 2, lo2[n]:],
                                              ALU.add).then_inc(s_r, 1)
                            dve.wait_ge(s_r, na + n_add[n])
                        if diag[n]:
                            dve.wait_ge(s_dm, nd + n_diag[n])
                        if n >= 2:
                            dve.wait_ge(s_arg, U + n - 1)
                        dve.tensor_copy(rh[:, n % 3, a:], r[:, a:]).then_inc(s_rh, 1)
                        dve.wait_ge(s_rh, U + n + 1)
                        dve.tensor_tensor(rl[:, n % 3, a:], r[:, a:], rh[:, n % 3, a:].bitcast(F32),
                                          ALU.subtract).then_inc(s_rl, 1)
                    if t in (5, 17):
                        Q = (5, 17).index(t)
                        dve.wait_ge(s_ga, 8 * i + 4 * Q + 3)
                        dve.scalar_tensor_tensor(out=raw_q[:, 1], in0=raw_q[:, 0], scalar=0.0, in1=raw_q[:, 1],
                                                 op0=ALU.min, op1=ALU.subtract).then_inc(s_gd, 1)
                    due(tiles_by(t - 1, 2), tiles_by(t, 2))

            with dve.Fori(0, NPAIR - 1) as i:
                sb_dve(i, N0 + 4 * i)
            sb_dve(NPAIR - 1, N0 + 4 * (NPAIR - 1))

            dve.wait_ge(s_la, 16)
            dve.tensor_tensor(la_d[:, 1:S], raw_la[:, 0:S - 1], raw_la[:, 1:S], ALU.subtract).then_inc(s_lo1, 1)
            dve.tensor_scalar(la_d[:, 0:1], raw_la[:, 0:1], -1.0, None, ALU.mult).then_inc(s_lo1, 1)
            dve.wait_ge(s_lo1, 2)
            dve.scalar_tensor_tensor(out=la[:, :], in0=la_d[:, :], scalar=vec("mu", 3 * NPAIR), in1=raw_la[:, 0:S],
                                     op0=ALU.mult, op1=ALU.add).then_inc(s_lo, 2)

            def rw_dve(i, p_):
                for h in range(2):
                    r = 2 * i + h

                    def due(point):
                        if p_ is not None:
                            split_upto(dve, split_low, panel_hi, p_, *rw_fill(h, point))

                    def pre(who, name):
                        after(dve, s_pre, PRE_STEPS, who, name, r)

                    def did(op):
                        op.then_inc(s_pre["dve"], 1)

                    if p_ is not None and h == 0:
                        split_upto(dve, split_low, panel_hi, p_, 0, 0)
                    t = [tt[:, m] for m in range(6)]
                    R, K, V = rkv[:, 0], rkv[:, 1], rkv[:, 2]
                    pcol = lambda m: pc[:, m:m + 1]
                    mu_v = vec_cols[:, vec_at["mu"]:vec_at["mu"] + 3 * NPAIR].rearrange("p (n b) -> p n b", b=NPAIR)
                    co_v = vec_cols[:, vec_at["w0"]:vec_at["w0"] + 7 * NPAIR].rearrange("p (n b) -> p n b", b=NPAIR)
                    did(dve.tensor_copy(pc[:, 0:3], mu_v[:, :, bass.ds(i, 1)].rearrange("p n b -> p (n b)")))
                    did(dve.tensor_copy(pc[:, 3:10], co_v[:, :, bass.ds(i, 1)].rearrange("p n b -> p (n b)")))
                    pre("dve", "c2")
                    did(dve.tensor_scalar(pc[:, 10:11], pc[:, 6:7], -1.0, 1.0, ALU.mult, ALU.add))
                    did(dve.memset(st[:, 0, :] if h == 0 else pc[:, 11:12], 0.0))
                    dve.wait_ge(s_rld, 48 * (r + 1))
                    if h == 0:
                        dve.wait_ge(s_z0, i + 1)
                    did(dve.tensor_tensor(rkv[:, :, :], ld[:, :, 3:3 + HALF], ld[:, :, 4:4 + HALF], ALU.subtract))
                    pre("dve", "d")
                    for m in range(3):
                        did(dve.scalar_tensor_tensor(out=rkv[:, m], in0=rkv[:, m], scalar=pcol(m), in1=ld[:, m, 4:4 + HALF],
                                                     op0=ALU.mult, op1=ALU.add))
                    pre("act", "w1")
                    did(dve.tensor_scalar(t[2], banks[4][:, :], pcol(3), 0.0, ALU.add, ALU.min))
                    pre("dve", "wm")
                    pre("act", "w3")
                    did(dve.tensor_tensor(t[0], t[2], t[0], ALU.subtract))
                    pre("act", "a1")
                    dve.wait_ge(s_yfree, 2 * r + 1)
                    did(dve.tensor_scalar(t[5], banks[5][:, :], pcol(4), 0.0, ALU.add, ALU.min))
                    pre("dve", "am")
                    pre("act", "a3")
                    did(dve.tensor_tensor(t[3], t[5], t[3], ALU.subtract))
                    due("pre1")
                    pre("act", "w4")
                    for c in range(HALF // CH):
                        op = dve.tensor_tensor_scan(t[1][:, c * CH:(c + 1) * CH], t[0][:, c * CH:(c + 1) * CH], zero_r[:, :],
                                                    0.0, ALU.add, ALU.add)
                    did(op)
                    pre("dve", "scan")
                    did(dve.tensor_tensor(t[0], t[1], t[0], ALU.subtract))
                    pre("act", "rn2")
                    did(dve.scalar_tensor_tensor(out=t[4], in0=K, scalar=pcol(5), in1=t[4], op0=ALU.mult, op1=ALU.mult))
                    pre("act", "Pp")
                    pre("dve", "kkn")
                    did(dve.tensor_tensor(t[0], t[4], t[0], ALU.mult))
                    pre("act", "a4")
                    did(dve.tensor_tensor(t[4], t[3], t[4], ALU.mult))
                    pre("act", "Pi")
                    pre("dve", "akk")
                    did(dve.tensor_tensor(t[4], t[4], t[1], ALU.mult))
                    did(dve.tensor_scalar(t[3], t[3], pcol(6), pcol(10), ALU.mult, ALU.add))
                    pre("dve", "kt")
                    did(dve.tensor_tensor(K, K, t[3], ALU.mult))
                    pre("dve", "k2")
                    did(dve.scalar_tensor_tensor(out=t[3], in0=R, scalar=pcol(7), in1=K, op0=ALU.mult, op1=ALU.mult))
                    did(dve.tensor_tensor(K, K, t[1], ALU.mult))
                    pre("act", "P")
                    did(dve.tensor_tensor(R, R, t[2], ALU.mult))
                    PC = t[2].rearrange("p (c t) -> p c t", t=CH)[:, :, CH - 1:CH].broadcast_to((P, HALF // CH, CH))
                    pre("dve", "Kh")
                    v3 = lambda a: a.rearrange("p (c t) -> p c t", t=CH)
                    did(dve.tensor_tensor(v3(t[1]), v3(K), PC, ALU.mult))
                    did(dve.tensor_tensor(v3(t[5]), v3(t[4]), PC, ALU.mult))
                    due("pre2")
                    pre("pe", "bs")
                    did(dve.tensor_tensor(t[3], banks[7][:, :], V, ALU.mult))
                    due("pre3")

                    def quad(who, name):
                        after(dve, s_quad, QUAD_STEPS, who, name, r)

                    def didq(op):
                        op.then_inc(s_quad["dve"], 1)

                    def mask(m):
                        return m_r[:, m:m + 1].broadcast_to((P, 4, P))

                    def gram(g, m):
                        return ps[:, 4 + 2 * g:6 + 2 * g, m % 2 * 2 * P:(m % 2 + 1) * 2 * P].rearrange("p e (b t) -> p e b t", t=P)

                    flat = lambda x: x.rearrange("p u t -> p (u t)")
                    by_head = lambda x: x.rearrange("p (e b) t -> p e b t", e=2)
                    mask4 = lambda m: m_r[:, m:m + 1].rearrange("p (a o) t -> p a o t", o=1).broadcast_to((P, 2, 2, P))
                    for g in range(2):
                        quad("pe", f"gB.{g}")
                        didq(dve.tensor_tensor(by_head(n_t[g]), gram(g, 0), mask4(M_STRICT), ALU.mult))
                        quad("dve", f"N.{g}")
                        didq(dve.tensor_tensor(u_i[:, g], n_t[g], mask(M_PAIR), ALU.mult))
                        quad("dve", f"n1.{g}")
                        didq(dve.tensor_tensor(u_i[:, g], ident[:, :].rearrange("p (o t) -> p o t", o=1).broadcast_to((P, 4, P)),
                                               u_i[:, g], ALU.subtract))
                        didq(dve.tensor_tensor(by_head(arb[:, g]), gram(g, 1), mask4(M_FULL), ALU.mult))
                        quad("dve", f"u.{g}")
                        didq(dve.transpose(flat(t_i[:, g]), flat(u_i[:, g])))
                    due("gram1")
                    for g in range(2):
                        quad("pe", f"gK.{g}")
                        didq(dve.tensor_tensor(by_head(aak[:, g]), gram(g, 2), mask4(M_STRICT), ALU.mult))
                        didq(dve.tensor_tensor(by_head(ark[:, g]), gram(g, 3), mask4(M_FULL), ALU.mult))
                    due("gram2")
                    due("tr")
                    for l in range(LV):
                        for g in range(2):
                            quad("pe", f"v{l}.{g}")
                            u_up = half_blocks(flat(u_i[:, g]), l, 1)
                            didq(dve.tensor_tensor(u_up, u_up, banks[5 + 2 * g][:, 0:HALF // 2].rearrange("p (c t) -> p c t", t=2 << l),
                                                   ALU.subtract))
                            if l < LV - 1:
                                quad("dve", f"u{l}.{g}")
                                didq(dve.transpose(flat(t_i[:, g]), flat(u_i[:, g])))
                        due(f"z{l}")
                        due(f"v{l}")
                    for g in range(2):
                        quad("act", f"uc.{g}")
                    def post(who, name):
                        after(dve, s_post, POST_STEPS, who, name, r)

                    def didp(op):
                        op.then_inc(s_post["dve"], 1)

                    g, gs = gate_r
                    for c in range(CHUNKS):
                        rows_ = slice(CH * (c % 2), CH * (c % 2) + CH)
                        tl = c // 2
                        quad("pe", f"sa{c}")
                        didq(dve.tensor_tensor(sa[rows_, tl], banks[4][rows_, 0:P], x_t[tl // 2][rows_, tl % 2], ALU.add))
                        quad("pe", f"st{c}")
                        tk = c * CH + CH - 1
                        for e in range(2):
                            h_ = slice(e * HD, e * HD + HD)
                            op = dve.scalar_tensor_tensor(out=st[h_, (c + 1) % 2, h_], in0=st[h_, c % 2, h_], scalar=t[2][h_, tk:tk + 1],
                                                          in1=banks[6][h_, h_], op0=ALU.mult, op1=ALU.add)
                        didq(op)
                        if c == 3:
                            post("act", "g3")
                            didp(dve.scalar_tensor_tensor(out=gs, in0=g, scalar=0.0, in1=gs, op0=ALU.min, op1=ALU.subtract))
                        if c == 5:
                            post("act", "g4")
                            didp(dve.tensor_tensor(gs, g, gs, ALU.mult))
                        due(f"c{c}")

                    post("pe", "m")
                    didp(dve.scalar_tensor_tensor(out=yb, in0=banks[4][:, :], scalar=-1.0 / HD, in1=yb,
                                                  op0=ALU.mult, op1=ALU.add))
                    due("m")
                    post("act", "e")
                    didp(dve.tensor_tensor(yb, yb, t[4], ALU.mult))
                    post("dve", "yn")
                    didp(dve.tensor_scalar(yb, yb, pcol(8), pcol(9), ALU.mult, ALU.add))
                    post("dve", "yw")
                    didp(dve.tensor_tensor(yb, yb, t[3], ALU.add))
                    post("dve", "yb")
                    didp(dve.tensor_tensor(yb, yb, gs, ALU.mult))
                    due("post")

            dve.wait_ge(s_mld, 16)
            dve.wait_ge(s_zr, 2)
            with dve.Fori(0, NPAIR - 1) as i:
                rw_dve(i, RW0 + 4 * i)
            rw_dve(NPAIR - 1, None)

            for s_, credit in ((s_ml, 2), (s_vl, 4), (s_h, 1), (s_pl, 1), (s_out, 4), (s_ev01, 4), (s_ev23, 4), (s_ss, 1), (s_sg, 1)):
                dve.nop().then_inc(s_, credit)
            with dve.Fori(0, 2) as h:
                def chunk_low(c):
                    dve.wait_ge(s_vh, h * NC + c + 1)
                    dve.tensor_tensor(vl[:, c % 2], v_raw[:, c % 4], vh[:, c % 2].bitcast(F32),
                                      ALU.subtract).then_inc(s_vl, 1)

                def panel(n):
                    where, m = (rows, n) if n < 4 else (ple, n - 4)
                    dve.wait_ge(s_vused, h * NC + LAST[n] + 1 + 2)
                    for b in range(2, HB):
                        dve.tensor_copy(where[:, b, m * HALF:(m + 1) * HALF],
                                        banks[4 * (n % 2) + b][:, :]).then_inc(s_ev23, 1)

                def sum_squares(which):
                    dve.wait_ge(s_ss, h * 32 + 16 * (which + 1) + 1)
                    dve.tensor_reduce(rs[:, which], ss[:, which], AX_X, ALU.add).then_inc(s_sum, 1)

                def residual(b):
                    dve.wait_ge(s_gb, 32)
                    dve.wait_ge(s_rs, 2 * h + 1)
                    dve.scalar_tensor_tensor(out=rows[:, b], in0=rows[:, b], scalar=rs[:, 0, b:b + 1], in1=g_post_b[:, :],
                                             op0=ALU.mult, op1=ALU.mult).then_inc(s_gain, 1)
                    dve.wait_ge(s_gain, 8 * h + b + 1)
                    dve.wait_ge(s_xr, 16 * (h * HB + b + 1))
                    dve.tensor_tensor(rows[:, b], rows[:, b], x_res[:, :], ALU.add).then_inc(s_h, 1)

                def gate(n, step):
                    cols = slice((n - 8) * HALF, (n - 7) * HALF)
                    on_act, done = h * 64 + 16 * (n - 8), h * 32 + 8 * (n - 8)
                    for b in range(HB):
                        if step == 0:
                            dve.wait_ge(s_sg, on_act + b + 1 + 1)
                            dve.tensor_scalar(sn[b], banks[4 * (n % 2) + b][:, :], 0.0, None,
                                              ALU.min).then_inc(s_ev01 if b < 2 else s_ev23, 1)
                        elif step == 1:
                            dve.wait_ge(s_ev01 if b < 2 else s_ev23, 2 * (h * NP_ + n) + b % 2 + 1 + 4)
                            dve.wait_ge(s_sg, on_act + 8 + b + 1 + 1)
                            dve.tensor_tensor(sn[b], sn[b], sg[b], ALU.subtract).then_inc(s_sgd, 1)
                        elif step == 2:
                            dve.wait_ge(s_sg, on_act + 12 + b + 1 + 1)
                            dve.tensor_tensor(sg[b], sg[b], ple[:, b, cols], ALU.mult).then_inc(s_sgd, 1)
                        else:
                            dve.wait_ge(s_sgd, done + 4 + b + 1)
                            dve.tensor_tensor(rows[:, b, cols], rows[:, b, cols], sg[b], ALU.add).then_inc(s_out, 1)

                for k in range(PLE // P):
                    dve.wait_ge(s_ph, h * 2 + k + 1)
                    dve.tensor_tensor(pl[:, k], banks[k][:, :], ph[:, k].bitcast(F32), ALU.subtract).then_inc(s_pl, 1)
                for m in range(KT // 2):
                    dve.wait_ge(s_mh, h * (KT // 2) + m + 1)
                    dve.tensor_tensor(al[:, 2 * m:2 * m + 2, :], m_in[:, m % 2], ah[:, 2 * m:2 * m + 2, :].bitcast(F32),
                                      ALU.subtract).then_inc(s_ml, 1)
                    chunk_low(m)
                dve.wait_ge(s_tick, h * 17 + 1)
                for c in range(KT // 2, NC):
                    chunk_low(c)
                    for step, at in ((1, 4), (2, 6), (3, 7)):
                        if c - at in LAST[8:]:
                            gate(LAST.index(c - at), step)
                    if c - 2 in LAST:
                        n = LAST.index(c - 2)
                        panel(n) if n < 8 else gate(n, 0)
                        if n == 3:
                            sum_squares(0)
                        if 3 <= n < 7:
                            residual(n - 3)
                        if n == 7:
                            sum_squares(1)
                            for k in range(KT):
                                dve.wait_ge(s_hh, h * KT + k + 1)
                                dve.tensor_tensor(al[:, k], banks[k % 4][:, :], ah[:, k].bitcast(F32),
                                                  ALU.subtract).then_inc(s_hl, 1)
                            for b in range(HB):
                                dve.wait_ge(s_rs, 2 * h + 2)
                                dve.scalar_tensor_tensor(out=ple[:, b], in0=ple[:, b], scalar=rs[:, 1, b:b + 1],
                                                         in1=g_ple_b[:, :], op0=ALU.mult, op1=ALU.mult).then_inc(s_gain, 1)
                            dve.wait_ge(s_gain, 8 * h + 8)
                for step in range(4):
                    gate(11, step)

        @block.tensor
        def _(pe):
            pe.wait_ge(s_ident, 1)
            pe.wait_ge(s_vec, 16 * len(vectors))
            pe.transpose(banks[4][:, 0:NVEC], vec_rows[:, :], ident[0:NVEC, 0:NVEC]).then_inc(s_vect, 1)
            for h in range(2):
                pe.wait_ge(s_xn, (h + 1) * HB)
                for k in range(KT):
                    need(pe, s_xl, h * KT + k - 3)
                    for b in range(HB):
                        mm = pe.transpose(banks[k % 4][:, b * P:(b + 1) * P], x_in[:, h * HB + b, k * P:(k + 1) * P],
                                          ident[:, :])
                    mm.then_inc(s_xt, 1)
            pe.wait_ge(s_xl, 2 * KT)

            for p_ in range(N0):
                for k in range(KT):
                    project_tile(pe, p_, p_ % 2, k)
            pe.wait_ge(s_c2, 2)

            def sb_pe(i, p_):
                U = NU * i
                tiles(pe, p_, 0, PRE_V)
                pe.wait_ge(s_qkv[2], 16 * (i + 1))
                for m in range(2):
                    for b in range(4):
                        mm = pe.transpose(banks[4 + m][:, b * P:(b + 1) * P],
                                          raw_v[:, (4 * m + b) * P:(4 * m + b + 1) * P], ident[:, :])
                    mm.then_inc(s_vt, 1)
                tiles(pe, p_, PRE_V, PRE)
                for t in range(SLOTS):
                    n = t
                    if n < NU:
                        Q, e, b = UNITS[n]
                        if n >= 3:
                            pe.wait_ge(s_ex, U + n - 2)
                        elif n == 0:
                            pe.wait_ge(s_tl, 4 * i + 4)
                        h_ = slice(e * HD, e * HD + HD)
                        for m, (kt, qt) in enumerate(((kh, qh), (kh, ql), (kl, qh))):
                            mm = pe.matmul(banks[4 + n % 3][:, lo[n]:], kt[h_, b * P:(b + 1) * P],
                                           qt[h_, Q * HALF + lo[n]:(Q + 1) * HALF], start=(m == 0), stop=(m == 2))
                        mm.then_inc(s_z, 1)
                    tiles(pe, p_, tiles_by(t - 1, 2), tiles_by(t, 0))
                    n = t - 3
                    if 0 <= n < NU:
                        Q, e, b = UNITS[n]
                        if first[n]:
                            need(pe, s_y, 4 * i + chain[n])
                        pe.wait_ge(s_al, U + n + 1)
                        for m, (vt, at) in enumerate(((vth, pah), (vth, pal), (vtl, pah))):
                            mm = pe.matmul(banks[7][:, lo[n]:], vt[:, b], at[:, n % 2, lo[n]:],
                                           start=(first[n] and m == 0), stop=(last[n] and m == 2), skip_group_check=True)
                        mm.then_inc(s_pv, 1)
                    tiles(pe, p_, tiles_by(t, 0), tiles_by(t, 1))
                    n = t - 1
                    if 0 <= n < NU:
                        pe.wait_ge(s_rl, U + n + 1)
                        bank = banks[4 + n % 3]
                        terms = [(c_r[:, 0], rh, n, lo[n]), (c_r[:, 0], rl, n, lo[n])]
                        if not first[n]:
                            terms += [(c_r[:, 1], rh, n - 1, lo2[n]), (c_r[:, 1], rl, n - 1, lo2[n])]
                        if diag[n]:
                            pe.matmul(bank[:, lo[n]:lo[n] + P], c_r[:, 3], c_r[:, 2], start=False, stop=False,
                                      skip_group_check=True)
                        for m, (ct, rt, j, a) in enumerate(terms):
                            mm = pe.matmul(bank[:, a:], ct, rt[:, j % 3, a:], start=False, stop=(m == len(terms) - 1),
                                           skip_group_check=True)
                        mm.then_inc(s_arg, 1)
                    tiles(pe, p_, tiles_by(t, 1), tiles_by(t, 2))

            with pe.Fori(0, NPAIR - 1) as i:
                sb_pe(i, N0 + 4 * i)
            sb_pe(NPAIR - 1, N0 + 4 * (NPAIR - 1))

            def rw_pe(i, p_):
                for h in range(2):
                    r = 2 * i + h

                    def fill(point):
                        if p_ is not None:
                            tiles(pe, p_, *rw_fill(h, point))

                    def pre(who, name):
                        after(pe, s_pre, PRE_STEPS, who, name, r)

                    t = [tt[:, m] for m in range(6)]
                    R, K, V = rkv[:, 0], rkv[:, 1], rkv[:, 2]
                    pe.wait_ge(s_lw, 32 * (i + 1))
                    pe.wait_ge(s_lo, 3)
                    for m in range(2):
                        h_ = slice(m * HD, m * HD + HD)
                        pe.matmul(banks[4 + m][:, :], lw[h_, :], la[h_, h * HALF:(h + 1) * HALF],
                                  start=True, stop=True).then_inc(s_pre["pe"], 1)
                    fill("pre1")
                    pre("act", "sq")
                    pe.matmul(banks[6][:, :], m_r[:, M_ONES], t[4], start=True, stop=True).then_inc(s_pre["pe"], 1)
                    fill("pre2")
                    pre("dve", "rk")
                    pe.matmul(banks[7][:, :], m_r[:, M_ONES], t[3], start=True, stop=True).then_inc(s_pre["pe"], 1)
                    fill("pre3")
                    pre("dve", "Rt")

                    def quad(who, name):
                        after(pe, s_quad, QUAD_STEPS, who, name, r)

                    def step(op):
                        op.then_inc(s_quad["pe"], 1)

                    units = [(u, u % 2, u // 2) for u in range(4)]

                    def cols(g, tl):
                        a = (2 * g + tl) * P
                        return slice(a, a + P)

                    def gram(g, m, lhs, rhs):
                        for u, tl, e in units:
                            h_ = slice(e * HD, e * HD + HD)
                            a = m % 2 * 2 * P + tl * P
                            mm = pe.matmul(banks[4 + 2 * g + e][:, a:a + P], lhs[h_, cols(g, tl)], rhs[h_, cols(g, tl)],
                                           start=True, stop=True)
                        step(mm)

                    for g in range(2):
                        if g:
                            pre("dve", "bon")
                        for m, rhs in enumerate((t[0], R)):
                            gram(g, m, t[4], rhs)
                    fill("gram1")
                    for m, (lhs, rhs) in enumerate(((K, t[0]), (K, R))):
                        for g in range(2):
                            quad("dve", f"B.{g}")
                            gram(g, m, lhs, rhs)
                    fill("gram2")
                    for m, pair in enumerate(((t[0], t[1]), (t[5], V))):
                        for g in range(2):
                            quad("dve", f"K.{g}")
                            for a, src in enumerate(pair):
                                for tl in range(2):
                                    mm = pe.transpose(banks[4 + 2 * g + m][:, (2 * a + tl) * P:(2 * a + tl + 1) * P],
                                                      src[:, cols(g, tl)], ident[:, :])
                            step(mm)

                    fill("tr")

                    def by_unit(g, tl, e):
                        return slice((2 * tl + e) * HD, (2 * tl + e + 1) * HD)

                    for g in range(2):
                        quad("act", f"tc2.{g}")
                        for u, tl, e in units:
                            mm = pe.matmul(banks[4 + 2 * g][:, by_unit(g, tl, e)], aak[:, g, u], t2_tok[g][:, 1, tl, e * HD:(e + 1) * HD],
                                           start=True, stop=True)
                        step(mm)
                    for l in range(LV):
                        for g in range(2):
                            if l == 0:
                                quad("act", f"xc.{g}")
                            quad("pool", f"nb{l}.{g}")
                            quad("dve", f"t{l - 1}.{g}" if l else f"t.{g}")
                            for u, _, _ in units:
                                mm = pe.matmul(banks[4 + 2 * g][:, u * CH:(u + 1) * CH], nb[:, g, u], half_blocks(t_i[:, g, u], l, 0),
                                               start=True, stop=True)
                            step(mm)
                        fill(f"z{l}")
                        for g in range(2):
                            quad("act", f"z{l}.{g}")
                            for u, _, _ in units:
                                mm = pe.matmul(banks[5 + 2 * g][:, u * CH:(u + 1) * CH], z_t[:, g, u], half_blocks(u_i[:, g, u], l, 1),
                                               start=True, stop=True)
                            step(mm)
                        fill(f"v{l}")
                    for g in range(2):
                        quad("dve", f"u{LV - 1}.{g}")
                        for u, tl, e in units:
                            mm = pe.matmul(banks[5 + 2 * g][e * HD:(e + 1) * HD, tl * P:(tl + 1) * P],
                                           t1_tok[g][:, 0, tl, e * HD:(e + 1) * HD], u_i[:, g, u], start=True, stop=True)
                        step(mm)
                    for g in range(2):
                        for u, tl, e in units:
                            mm = pe.matmul(banks[4 + 2 * g][:, by_unit(g, tl, e)], u_i[:, g, u], x_t[g][:, tl, e * HD:(e + 1) * HD],
                                           start=True, stop=True)
                        step(mm)
                    for g in range(2):
                        quad("act", f"wc.{g}")
                        quad("act", f"uc.{g}")
                    for c in range(CHUNKS):
                        g, tl, pp = c // 4, c // 2 % 2, c % 2
                        tr = slice(CH * pp, CH * pp + CH)
                        yt = banks[5 + 2 * g]
                        if c:
                            quad("dve", f"st{c - 1}")
                        step(pe.matmul(banks[4][tr, 0:P], wt[g][:, tl, tr], st[:, c % 2], start=True, stop=True))
                        pe.matmul(banks[6][:, 0:P], t1_tok[g][tr, 1, tl], t2_tok[g][tr, 1, tl], start=True, stop=False)
                        if pp == 0:
                            for e in range(2):
                                pe.matmul(yt[e * HD:(e + 1) * HD, tl * P:(tl + 1) * P], t2_tok[g][:, 1, tl, e * HD:(e + 1) * HD],
                                          ark[:, g, tl + 2 * e], start=True, stop=False, skip_group_check=True)
                        quad("dve", f"sa{c}")
                        step(pe.matmul(banks[6][:, 0:P], t2_tok[g][tr, 0, tl], sa[tr, c // 2], start=False, stop=True))
                        pe.matmul(yt[:, c % 4 * CH:(c % 4 + 1) * CH], st[:, c % 2], R[:, c * CH:(c + 1) * CH],
                                  start=False, stop=False, skip_group_check=True)
                        if pp == 1:
                            for e in range(2):
                                mm = pe.matmul(yt[e * HD:(e + 1) * HD, tl * P:(tl + 1) * P], sa[:, c // 2, e * HD:(e + 1) * HD],
                                               arb[:, g, tl + 2 * e], start=False, stop=True, skip_group_check=True)
                            if tl == 1:
                                step(mm)
                        fill(f"c{c}")

                    after(pe, s_quad, QUAD_STEPS, "act", "y.1", r)
                    pe.matmul(banks[4][:, :], m_r[:, M_ONES], yb, start=True, stop=True).then_inc(s_post["pe"], 1)
                    fill("m")
                    after(pe, s_post, POST_STEPS, "act", "q", r)
                    pe.matmul(banks[5][:, :], m_r[:, M_ONES], t[4], start=True, stop=True).then_inc(s_post["pe"], 1)
                    fill("post")
                    after(pe, s_post, POST_STEPS, "dve", "yc", r)
                    after(pe, s_post, POST_STEPS, "act", "l", r)

            pe.wait_ge(s_mld, 16)
            pe.wait_ge(s_zr, 2)
            with pe.Fori(0, NPAIR - 1) as i:
                rw_pe(i, RW0 + 4 * i)
            rw_pe(NPAIR - 1, None)

            pe.nop().then_inc(s_vused, 2)
            with pe.Fori(0, 2) as h:
                def chunk(c, n, k0, kt, hi, lo):
                    if k0 == 0:
                        pe.wait_ge(s_ev01, 2 * (h * NP_ + n) + 2)
                        pe.wait_ge(s_ev23, 2 * (h * NP_ + n) + 2)
                    pe.wait_ge(s_vl, h * NC + c + 1 + 4)
                    for k2 in range(2):
                        for m, (at, wt) in enumerate(((hi, vh), (hi, vl), (lo, vh))):
                            for b in range(HB):
                                mm = pe.matmul(banks[4 * (n % 2) + b][:, :], at[:, k0 + k2, b * P:(b + 1) * P],
                                               wt[:, c % 2, k2], start=(k0 + k2 == 0 and m == 0),
                                               stop=(k0 + k2 == kt - 1 and m == 2))
                    mm.then_inc(s_vused, 1)

                pe.wait_ge(s_p, 16 * (h + 1))
                pe.wait_ge(s_ev01, 2 * h * NP_ + 4)
                for k in range(PLE // P):
                    for b in range(HB):
                        mm = pe.transpose(banks[k][:, b * P:(b + 1) * P], p_in[:, b, k * P:(k + 1) * P], ident[:, :])
                    mm.then_inc(s_pt, 1)
                pe.wait_ge(s_pl, h * 2 + 2 + 1)
                for c in range(32):
                    if c < 8:
                        pe.wait_ge(s_ml, h * (KT // 2) + c + 1 + 2)
                    chunk(c, c // 8, c % 8 * 2, KT, ah, al)
                for c in range(32, 36):
                    chunk(c, c - 28, 0, 2, ph, pl)
                pe.wait_ge(s_h, h * HB + HB + 1)
                for k in range(KT):
                    if k == 0:
                        pe.wait_ge(s_ev01, 2 * (h * NP_ + 7) + 4)
                        pe.wait_ge(s_ev23, 2 * (h * NP_ + 7) + 4)
                    if k >= 4:
                        pe.wait_ge(s_hl, h * KT + k - 3)
                    for b in range(HB):
                        mm = pe.transpose(banks[k % 4][:, b * P:(b + 1) * P], rows[:, b, k * P:(k + 1) * P], ident[:, :])
                    mm.then_inc(s_ht, 1)
                pe.wait_ge(s_hl, h * KT + KT)
                for c in range(36, NC):
                    chunk(c, 8 + (c - 36) // 8, (c - 36) % 8 * 2, KT, ah, al)


_INS = ["x", "p", "g_pre", "w_in", "mu_shift", "w0", "w_up", "a0", "a_up", "k_k", "k_a", "r_k",
        "lnx_w", "lnx_b", "w_out", "g_post", "w_ple", "w_plg", "g_ple"]


def kernel(**inputs):
    import concourse.bacc as bacc
    from concourse.bass_utils import run_bass_kernel_spmd

    nc = bacc.Bacc("TRN2", target_bir_lowering=False, num_devices=1)
    arrays, args = {}, []
    for name in _INS:
        a = np.ascontiguousarray(inputs[name])
        arrays[f"in_{name}"] = a
        args.append(nc.dram_tensor(f"in_{name}", a.shape, mybir.dt.from_np(a.dtype), kind="ExternalInput").ap())
    shape = tuple(inputs["x"].shape)
    out = nc.dram_tensor("layer_out", shape, F32, kind="ExternalOutput").ap()
    layer_kernel(nc, *args, out)
    r = run_bass_kernel_spmd(nc, [arrays], core_ids=[0])
    return r.results[0]["layer_out"]
```
